# Optimizing a Trainium2 kernel written in Bass

```python
import jax, jax.numpy as jnp
from jax import lax
import numpy as np

D_MODEL = 1024
BATCH = 1
SEQ = 512
DEPTH = 1
DEC_BATCH = 8
DEC_SEQ = 4
PAST_LEN = 2048
PAGE_SIZE = 128

CONV_W = D_MODEL // 2
CONV_K = 3
HEAD_DIM = 64
N_HEADS = (D_MODEL // 2) // HEAD_DIM
N_KV = 2
GROUP = N_HEADS // N_KV
ATT_W = N_HEADS * HEAD_DIM
KV_W = N_KV * HEAD_DIM
WINDOW = 128
Q_BLOCK = WINDOW
ATT_SCALE = HEAD_DIM ** -0.5
N_BRANCH = 2
IN_W = 3 * CONV_W + ATT_W + 2 * KV_W + N_BRANCH * D_MODEL
N_EXPERTS = 32
TOP_K = 4
D_FF = D_MODEL
SWIGLU_ALPHA = 1.702
SWIGLU_LIMIT = 7.0
MOE_BLOCK = 128
PLE_DIM = 256
RMS_EPS = 1e-5

kernel_name = "hybrid_gated_conv_swa_moe_step"

def _rmsnorm(x, g):
    xf = x.astype(jnp.float32)
    r = lax.rsqrt(jnp.mean(xf * xf, axis=-1, keepdims=True) + RMS_EPS)
    return (xf * r * g.astype(jnp.float32)).astype(x.dtype)

def _alibi_slopes():
    h = jnp.arange(1, N_HEADS + 1, dtype=jnp.float32)
    return jnp.exp2(-8.0 * h / N_HEADS).reshape(N_KV, GROUP)

def _short_conv(u, prev, conv_w):
    up = jnp.concatenate([prev, u], axis=1)
    T = u.shape[1]
    y = sum(conv_w[j] * up[:, j:j + T] for j in range(CONV_K))
    return y, up[:, -(CONV_K - 1):]

def _window_attend(q, k, v, q_pos, k_pos, sinks):
    s = jnp.einsum('bnqhgd,bnkhd->bnhgqk', q, k, preferred_element_type=jnp.float32) * ATT_SCALE
    dist = q_pos[:, :, None] - k_pos[:, None, :]
    valid = (dist >= 0) & (dist < WINDOW) & (k_pos[:, None, :] >= 0)
    s = s - _alibi_slopes()[:, :, None, None] * dist[:, None, None].astype(jnp.float32)
    s = jnp.where(valid[:, None, None], s, -jnp.inf)
    sink = sinks.astype(jnp.float32).reshape(N_KV, GROUP)[:, :, None, None]
    m = jnp.maximum(jnp.max(s, axis=-1, keepdims=True), sink)
    p = jnp.exp(s - m)
    denom = jnp.sum(p, axis=-1, keepdims=True) + jnp.exp(sink - m)
    o = jnp.einsum('bnhgqk,bnkhd->bnqhgd', p / denom, v.astype(jnp.float32))
    return o.astype(q.dtype)

def _attn_prompt(q, k, v, sinks, wb):
    B, S = q.shape[:2]
    nb = S // Q_BLOCK
    qb = q.reshape(B, nb, Q_BLOCK, N_KV, GROUP, HEAD_DIM)

    def band(t):
        tp = jnp.concatenate([jnp.zeros((B, WINDOW) + t.shape[2:], t.dtype), t], axis=1)
        tp = tp.reshape((B, nb + 1, Q_BLOCK) + t.shape[2:])
        return jnp.concatenate([tp[:, :-1], tp[:, 1:]], axis=2)

    q_pos = jnp.arange(S, dtype=jnp.int32).reshape(nb, Q_BLOCK)
    kp = jnp.arange(-WINDOW, S, dtype=jnp.int32).reshape(nb + 1, Q_BLOCK)
    k_pos = jnp.concatenate([kp[:-1], kp[1:]], axis=1)
    o = _window_attend(qb, band(k), band(v), q_pos, k_pos, sinks)
    return o.reshape(B, S, ATT_W), k[:, S - wb:], v[:, S - wb:]

def _attn_sample(q, k, v, k_prev, v_prev, sinks):
    N, T = q.shape[:2]
    wb = k_prev.shape[1]
    kk = jnp.concatenate([k_prev, k], axis=1)
    vv = jnp.concatenate([v_prev, v], axis=1)
    q_pos = PAST_LEN + jnp.arange(T, dtype=jnp.int32)
    k_pos = PAST_LEN - wb + jnp.arange(wb + T, dtype=jnp.int32)
    o = _window_attend(q[:, None], kk[:, None], vv[:, None], q_pos[None], k_pos[None], sinks)
    return o.reshape(N, T, ATT_W), kk[:, -wb:], vv[:, -wb:]

def _mixer(a, conv_prev, kv_prev, wb, w_in, conv_w, sinks, w_branch, w_out):
    N, T, _ = a.shape
    z = a @ w_in
    cuts = [CONV_W, 2 * CONV_W, 3 * CONV_W, 3 * CONV_W + ATT_W,
            3 * CONV_W + ATT_W + KV_W, 3 * CONV_W + ATT_W + 2 * KV_W]
    bg, cg, hc, q, k, v, gl = jnp.split(z, cuts, axis=-1)
    yc, conv_new = _short_conv(cg * hc, conv_prev, conv_w)
    yc = bg * yc
    q = q.reshape(N, T, N_KV, GROUP, HEAD_DIM)
    k = k.reshape(N, T, N_KV, HEAD_DIM)
    v = v.reshape(N, T, N_KV, HEAD_DIM)
    if kv_prev is None:
        ya, k_new, v_new = _attn_prompt(q, k, v, sinks, wb)
    else:
        ya, k_new, v_new = _attn_sample(q, k, v, kv_prev[0], kv_prev[1], sinks)
    yb = jnp.einsum('rntc,rcd->rntd', jnp.stack([yc, ya]), w_branch)
    gates = jax.nn.sigmoid(jnp.moveaxis(gl.reshape(N, T, N_BRANCH, D_MODEL), 2, 0).astype(jnp.float32))
    merged = jnp.sum(gates * yb.astype(jnp.float32), axis=0).astype(a.dtype)
    return merged @ w_out, conv_new, k_new, v_new

def _moe(x, w_router, b_router, w_up, b_up, w_down, b_down):
    T, D = x.shape
    logits = x.astype(jnp.float32) @ w_router.astype(jnp.float32) + b_router.astype(jnp.float32)
    top_v, top_i = lax.top_k(logits, TOP_K)
    gate = jax.nn.softmax(top_v, axis=-1)
    A = T * TOP_K
    flat_e = top_i.reshape(-1).astype(jnp.int32)
    order = jnp.argsort(flat_e)
    sorted_e = flat_e[order]
    sorted_tok = (order // TOP_K).astype(jnp.int32)
    counts = jnp.bincount(flat_e, length=N_EXPERTS).astype(jnp.int32)
    padded = (counts + MOE_BLOCK - 1) // MOE_BLOCK * MOE_BLOCK
    pad_end = jnp.cumsum(padded)
    pad_start = pad_end - padded
    start = jnp.cumsum(counts) - counts
    slot = pad_start[sorted_e] + (jnp.arange(A, dtype=jnp.int32) - start[sorted_e])
    n_blocks = -(-A // MOE_BLOCK) + N_EXPERTS
    P = n_blocks * MOE_BLOCK
    slot_tok = jnp.full((P,), T, jnp.int32).at[slot].set(sorted_tok)
    x_pad = jnp.concatenate([x, jnp.zeros((1, D), x.dtype)], axis=0)
    xs = x_pad[slot_tok].reshape(n_blocks, MOE_BLOCK, D)
    block_e = jnp.minimum(
        jnp.searchsorted(pad_end, jnp.arange(n_blocks, dtype=jnp.int32) * MOE_BLOCK, side='right'),
        N_EXPERTS - 1).astype(jnp.int32)

    def expert_block(args):
        xb, e = args
        h = (xb @ w_up[e] + b_up[e]).reshape(MOE_BLOCK, D_FF, 2)
        x_glu = jnp.minimum(h[..., 0], SWIGLU_LIMIT)
        x_lin = jnp.clip(h[..., 1], -SWIGLU_LIMIT, SWIGLU_LIMIT)
        act = x_glu * jax.nn.sigmoid(SWIGLU_ALPHA * x_glu) * (x_lin + 1)
        return act @ w_down[e] + b_down[e]

    ys = lax.map(expert_block, (xs, block_e)).reshape(P, D)
    slot_of = jnp.zeros((A,), jnp.int32).at[order].set(slot)
    y = ys[slot_of].reshape(T, TOP_K, D)
    return jnp.einsum('tk,tkd->td', gate.astype(y.dtype), y)

def _ple(h, p, g, w_gate, w_proj):
    gate = jax.nn.sigmoid((_rmsnorm(h, g) @ w_gate).astype(jnp.float32))
    return h + (gate * (p @ w_proj).astype(jnp.float32)).astype(h.dtype)

def setup_inputs(seed: int = 0) -> dict:
    key = jax.random.key(seed)
    ks = jax.random.split(key, 32)
    f32 = jnp.float32
    wb = min(WINDOW, PAST_LEN)
    nrm = lambda k, shape, s: jax.random.normal(k, shape, f32) * s
    gain = lambda k, shape: 1.0 + 0.01 * jax.random.normal(k, shape, f32)
    return {
        "x_prompt": nrm(ks[0], (BATCH, SEQ, D_MODEL), 1.0),
        "x_sample": nrm(ks[1], (DEC_BATCH, DEC_SEQ, D_MODEL), 1.0),
        "state_conv": nrm(ks[2], (DEPTH, DEC_BATCH, CONV_K - 1, CONV_W), 0.5),
        "cache_k": nrm(ks[3], (DEPTH, DEC_BATCH, wb, N_KV, HEAD_DIM), 1.0),
        "cache_v": nrm(ks[4], (DEPTH, DEC_BATCH, wb, N_KV, HEAD_DIM), 1.0),
        "p_prompt": nrm(ks[5], (DEPTH, BATCH, SEQ, PLE_DIM), 1.0),
        "p_sample": nrm(ks[6], (DEPTH, DEC_BATCH, DEC_SEQ, PLE_DIM), 1.0),
        "g_mix": gain(ks[7], (DEPTH, D_MODEL)),
        "w_in": nrm(ks[8], (DEPTH, D_MODEL, IN_W), D_MODEL ** -0.5),
        "conv_w": nrm(ks[9], (DEPTH, CONV_K, CONV_W), CONV_K ** -0.5),
        "sinks": nrm(ks[10], (DEPTH, N_HEADS), 0.5),
        "w_branch": nrm(ks[11], (DEPTH, N_BRANCH, CONV_W, D_MODEL), CONV_W ** -0.5),
        "w_out": nrm(ks[12], (DEPTH, D_MODEL, D_MODEL), D_MODEL ** -0.5),
        "g_ffn": gain(ks[13], (DEPTH, D_MODEL)),
        "w_router": nrm(ks[14], (DEPTH, D_MODEL, N_EXPERTS), D_MODEL ** -0.5),
        "b_router": nrm(ks[15], (DEPTH, N_EXPERTS), 0.01),
        "w_up": nrm(ks[16], (DEPTH, N_EXPERTS, D_MODEL, 2 * D_FF), D_MODEL ** -0.5),
        "b_up": nrm(ks[17], (DEPTH, N_EXPERTS, 2 * D_FF), 0.01),
        "w_down": nrm(ks[18], (DEPTH, N_EXPERTS, D_FF, D_MODEL), D_FF ** -0.5),
        "b_down": nrm(ks[19], (DEPTH, N_EXPERTS, D_MODEL), 0.01),
        "g_ple": gain(ks[20], (DEPTH, D_MODEL)),
        "w_ple_gate": nrm(ks[21], (DEPTH, D_MODEL, D_MODEL), D_MODEL ** -0.5),
        "w_ple": nrm(ks[22], (DEPTH, PLE_DIM, D_MODEL), PLE_DIM ** -0.5),
        "g_final": gain(ks[23], (D_MODEL,)),
    }

def reference(x_prompt, x_sample, state_conv, cache_k, cache_v, p_prompt, p_sample,
              g_mix, w_in, conv_w, sinks, w_branch, w_out, g_ffn, w_router, b_router,
              w_up, b_up, w_down, b_down, g_ple, w_ple_gate, w_ple, g_final):
    hp, hs = x_prompt, x_sample
    Bp, Sp, _ = hp.shape
    n_prompt = Bp * Sp
    wb = cache_k.shape[2]
    conv_p, conv_s, k_p, v_p, k_s, v_s = [], [], [], [], [], []
    for i in range(DEPTH):
        ap = _rmsnorm(hp, g_mix[i])
        as_ = _rmsnorm(hs, g_mix[i])
        zero_prev = jnp.zeros((Bp, CONV_K - 1, CONV_W), ap.dtype)
        op, cp, kp, vp = _mixer(ap, zero_prev, None, wb, w_in[i], conv_w[i], sinks[i], w_branch[i], w_out[i])
        os_, cs, ks_, vs_ = _mixer(as_, state_conv[i], (cache_k[i], cache_v[i]), wb,
                                   w_in[i], conv_w[i], sinks[i], w_branch[i], w_out[i])
        hp = hp + op
        hs = hs + os_
        m_all = jnp.concatenate([_rmsnorm(hp, g_ffn[i]).reshape(-1, D_MODEL),
                                 _rmsnorm(hs, g_ffn[i]).reshape(-1, D_MODEL)], axis=0)
        y_all = _moe(m_all, w_router[i], b_router[i], w_up[i], b_up[i], w_down[i], b_down[i])
        hp = hp + y_all[:n_prompt].reshape(hp.shape)
        hs = hs + y_all[n_prompt:].reshape(hs.shape)
        hp = _ple(hp, p_prompt[i], g_ple[i], w_ple_gate[i], w_ple[i])
        hs = _ple(hs, p_sample[i], g_ple[i], w_ple_gate[i], w_ple[i])
        conv_p.append(cp); conv_s.append(cs)
        k_p.append(kp); v_p.append(vp); k_s.append(ks_); v_s.append(vs_)
    y_prompt = _rmsnorm(hp, g_final)
    y_sample = _rmsnorm(hs, g_final)
    return (y_prompt, y_sample, jnp.stack(conv_p), jnp.stack(conv_s),
            jnp.stack(k_p), jnp.stack(v_p), jnp.stack(k_s), jnp.stack(v_s))


_drawn_inputs = setup_inputs


def setup_inputs(seed=0):
    import zlib

    import numpy as np

    out = dict(_drawn_inputs(seed))
    spreads = {}
    factors = {'b_up': 8.0, 'b_down': 8.0, 'g_ple': 200.0, 'g_final': 196.224}
    for name, (base, spread) in spreads.items():
        noise = np.random.default_rng([zlib.crc32(name.encode()), seed]).standard_normal(out[name].shape)
        drawn = base * np.exp(spread * noise) if base else spread * noise
        out[name] = __import__('jax').numpy.asarray(drawn.astype(out[name].dtype))
    for name, factor in factors.items():
        out[name] = (out[name] * factor).astype(out[name].dtype)
    return out
```

```python
from contextlib import ExitStack

import numpy as np
import concourse.bass as bass
from concourse import mybir

F32 = mybir.dt.float32
F32R = mybir.dt.float32r
I32 = mybir.dt.int32
U32 = mybir.dt.uint32
ALU = mybir.AluOpType
ACT = mybir.ActivationFunctionType
AX_X = mybir.AxisListType.X

P = 128
D = 1024
KT = D // P
SEQ = 512
NSEQ, TDEC = 8, 4
TS = NSEQ * TDEC
T = SEQ + TS
NT = 5
ROWS = [P, P, P, P, TS]
HALF = T // 2
CW = 512
CT = CW // P
NH, NKV, HD = 8, 2, 64
GRP = NH // NKV
WIN = 128
SCALE = HD ** -0.5
NEXP, TOPK = 32, 4
FF = D
PLE = 256
EPS = 1e-5
ALPHA, LIMIT = 1.702, 7.0
SLOPE = [2.0 ** (-8.0 * (h + 1) / NH) for h in range(NH)]

CH = 2048
PP_SLOT = [0, 1, 3, 0, 1]
RAW_MIX, RAW = 4, 6
SPL_MIX, SPL = 2, 3
Z_CHUNKS = 9
PAIRS = 4
BR_CHUNKS = 3 * PAIRS
WO_CHUNKS = 4
WO_COL = [0, 2, 1, 3]
NM = Z_CHUNKS + BR_CHUNKS + WO_CHUNKS
UPC, DNC = 8, 4
BLK = UPC + DNC
PEEL = 3
MAXOVER = 16
ROWS_DUMP = T + P
PLE_CHUNKS = 5


def tiles_after(c):
    return 2 * (c + 1)


TB = tiles_after(Z_CHUNKS + BR_CHUNKS - 1) + NT
ROUT = 8
R0S = 5
NORMS = [("in", 0), ("in", 1), ("in", 2), ("out", 0), ("in", 3), ("out", 1), ("in", 4), ("out", 2), ("out", 3), ("out", 4)]


def build(nc, A, O):
    with ExitStack() as ctx:
        def sem(name):
            return ctx.enter_context(nc.semaphore(name))

        SB0 = (nc.sbuf_base + 31) // 32 * 32
        nc.alloc_sbuf_tensor("slab", [P, 212800 // 4], F32)

        def at(name, shape, dt, off):
            n = int(np.prod(shape[1:])) * 4
            assert off + n <= 212800, (name, off + n)
            return nc.alloc_sbuf_tensor_at(name, shape, dt, offset=SB0 + off)

        CB = CH * 4
        raw = [at(f"raw{s}", [P, CH], F32, (s if s < 4 else s + 4) * CB) for s in range(RAW)]
        wh = [at(f"wh{s}", [P, CH], F32R, (4 + s if s < 2 else 10) * CB) for s in range(SPL)]
        wl = [at(f"wl{s}", [P, CH], F32R, (6 + s if s < 2 else 11) * CB) for s in range(SPL)]
        XA, XB = 8 * CB, 10 * CB
        R0 = 12 * CB
        R1 = R0 + 2 * KT * T * 4
        R2 = R1 + 2 * KT * T * 4
        RC = R2 + 39680
        aTh = at("aTh", [P, KT, T], F32R, R0)
        aTl = at("aTl", [P, KT, T], F32R, R0 + KT * T * 4)
        yTh = at("yTh", [P, 2 * CT, T], F32R, R1)
        yTl = at("yTl", [P, 2 * CT, T], F32R, R1 + KT * T * 4)
        xin = at("xin", [P, NT, D], F32, R1)
        brow = at("brow", [NEXP, 3 * D], F32, R1 + NT * D * 4)
        bhi = at("bhi", [NEXP, 3 * D], F32R, XA)
        blo = at("blo", [NEXP, 3 * D], F32R, XB)
        ckrow = at("ckrow", [P, NSEQ, P], F32, XA + 12288)
        ksT = at("ksT", [P, NSEQ, P], F32, XB)
        vc = at("vc", [P, NSEQ, P], F32, XB + 12288)
        Ss = at("Ss", [P, 2, 160], F32, XB + 4096)
        PsT = at("PsT", [P, 2, P], F32, XB + 5376)
        PsN = at("PsN", [TS, 2, P], F32, XB + 6400)
        crow = at("crow", [18, CW], F32, XB + 7424)
        strow = at("strow", [16, CW], F32, R1 + 32768)
        S = at("S", [P, NH, 256], F32, XA)
        PT = at("PT", [P, 2 * NH, P], F32, XA + 8192)
        off = R2
        upP = at("upP", [P, CT, SEQ + 2], F32, off); off += (CT * (SEQ + 2) * 4 + 31) // 32 * 32
        upS = at("upS", [P, CT, NSEQ, TDEC + 2], F32, off); off += (CT * NSEQ * 6 * 4 + 31) // 32 * 32
        gmix = at("gmix", [P, D], F32, off)
        cv = at("cv", [P, CT, T], F32, off); off += (CT * T * 4 + 31) // 32 * 32
        qTh = at("qTh", [P, CT, SEQ], F32R, off); off += CT * SEQ * 4
        qS = at("qS", [P, CT, TS], F32, off); off += CT * TS * 4
        qTl = at("qTl", [P, CT, SEQ], F32R, R1 + KT * T * 4)
        kTh = at("kTh", [P, SEQ], F32R, R1)
        kTl = at("kTl", [P, SEQ], F32R, R1 + T * 4)
        kvT = at("kvT", [P, 2, T], F32, off); off += (2 * T * 4 + 31) // 32 * 32
        vrow = at("vrow", [P, NT, P], F32, off); off += (NT * P * 4 + 31) // 32 * 32
        qbd = at("qbd", [P, NSEQ, 2 * NSEQ * 2], F32, off); off += (NSEQ * 32 * 4 + 31) // 32 * 32
        off = max(off, R2 + 2 * KT * T * 4)
        cst = at("cst", [P, CT, 18], F32, off); off += (CT * 18 * 4 + 31) // 32 * 32
        krow = at("krow", [P, 2, P], F32, off); off += (2 * P * 4 + 31) // 32 * 32
        assert off <= RC
        mTh = at("mTh", [P, KT, T], F32R, R2)
        mTl = at("mTl", [P, KT, T], F32R, R2 + KT * T * 4)
        sg = at("sg", [P, 2, 2, T], F32, XA)
        wo_h = [wh[1], wh[2], wh[0], at("wo_h3", [P, CH], F32R, 8 * CB)]
        wo_l = [wl[1], wl[2], wl[0], at("wo_l3", [P, CH], F32R, 9 * CB)]
        hrow = at("hrow", [P, NT, D], F32, R0)
        mrow = at("mrow", [P, NT, D], F32, R1)
        gffn = at("gffn", [P, D], F32, R1 + 20480)
        wr = at("wr", [P, KT, NEXP], F32, R1 + 24576)
        brt = at("brt", [P, NEXP], F32, R1 + 25600)
        mTf = at("mTf", [P, 2, KT * P], F32, R1 + 26112)
        off = R0 + 20480
        lg = at("lg", [P, NT, NEXP], F32, off); off += (NT * NEXP * 4 + 31) // 32 * 32
        top = at("top", [P, NT, 8], F32, off); off += (NT * 32 + 31) // 32 * 32
        topi = at("topi", [P, NT, 8], U32, off); off += (NT * 32 + 31) // 32 * 32
        topf = at("topf", [P, NT, TOPK], F32, off); off += (NT * 16 + 31) // 32 * 32
        ev = at("ev", [P, NT, TOPK], F32, off); off += (NT * 16 + 31) // 32 * 32
        esum = at("esum", [P, NT], F32, off); off += (32 + 31) // 32 * 32
        ersum = at("ersum", [P, NT], F32, off); off += (32 + 31) // 32 * 32
        oneh = at("oneh", [P, NT * TOPK, NEXP], F32, off); off += (NT * TOPK * NEXP * 4 + 31) // 32 * 32
        mask = at("mask", [P, NT, NEXP], F32, off); off += (NT * NEXP * 4 + 31) // 32 * 32
        rankm = at("rankm", [P, NT, NEXP], F32, off); off += (NT * NEXP * 4 + 31) // 32 * 32
        gate = at("gate", [P, NT, NEXP], F32, off); off += (NT * NEXP * 4 + 31) // 32 * 32
        before = at("before", [P, NT, NEXP], F32, off); off += (NT * NEXP * 4 + 31) // 32 * 32
        all4 = at("all4", [P, 4, NEXP], F32, off); off += (4 * NEXP * 4 + 31) // 32 * 32
        over = at("over", [P, 2], F32, off); off += (32 + 31) // 32 * 32
        pos = at("pos", [P, 1], F32, off); off += (32 + 31) // 32 * 32
        oh16 = at("oh16", [P, MAXOVER], F32, off); off += (64 + 31) // 32 * 32
        tabE = at("tabE", [1, 64], I32, off); off += (256 + 31) // 32 * 32
        tabB = at("tabB", [1, 64], I32, off); off += (256 + 31) // 32 * 32
        tabN = at("tabN", [1, 8], I32, off); off += (32 + 31) // 32 * 32
        assert off <= R1
        xTh = at("xTh", [P, KT, P], F32R, R0)
        xTl = at("xTl", [P, KT, P], F32R, R0 + 4096)
        xg = at("xg", [P, D], F32, R0 + 8192)
        gl = at("gl", [P, 2, FF], F32, R1)
        sgm = at("sgm", [P, FF], F32, R1 + 8192)
        arow = at("arow", [P, FF], F32, R1 + 12288)
        acTh = at("acTh", [P, KT, P], F32R, R1 + 16384)
        acTl = at("acTl", [P, KT, P], F32R, R1 + 20480)
        yrow = at("yrow", [P, D], F32, R1 + 24576)
        Rsel = at("Rsel", [P, NT, P], F32, R2)
        iota = at("iota", [P, NT * P], F32, R2 + 2560)
        bup = at("bup", [2, 2 * FF], F32R, R2 + 5120)
        bdn = at("bdn", [2, D], F32R, R2 + 13824)
        nTh = at("nTh", [P, KT, T], F32R, R1)
        nTl = at("nTl", [P, KT, T], F32R, R1 + KT * T * 4)
        pp = at("pp", [P, NT, D], F32, R2 + 17920)
        prow = at("prow", [P, NT, PLE], F32, R2)
        pTh = at("pTh", [P, 2, T], F32R, R2 + 5120)
        pTl = at("pTl", [P, 2, T], F32R, R2 + 9472)
        xnb = at("xnb", [P, 3, D], F32, R2 + 5120)
        gfin = at("gfin", [P, D], F32, R2)
        gple = at("gple", [P, D], F32, R0 + 20480)
        gate_h = [wh[2], wh[0], at("gate_h2", [P, CH], F32R, 3 * CB), wh[1]]
        gate_l = [wl[2], wl[0], at("gate_l2", [P, CH], F32R, 8 * CB), wl[1]]
        off = RC

        def small(name, shape, dt=F32):
            nonlocal off
            t = at(name, shape, dt, off)
            off += (int(np.prod(shape[1:])) * 4 + 31) // 32 * 32
            return t

        ident = small("ident", [P, P])
        negd = small("negd", [P, 256])
        biass = small("biass", [P, 2, 160])
        sinkb = small("sinkb", [P, NH])
        sinks_s = small("sinks_s", [P, 1])
        cwT = small("cwT", [P, 3, CT])
        epsb = small("epsb", [P, 1])
        ss = small("ss", [P, 8])
        std = small("std", [P, 8])
        rinv = small("rinv", [P, 8])
        mx = small("mx", [P, NH])
        mm = small("mm", [P, NH])
        negm = small("negm", [P, NH])
        esi = small("esi", [P, NH])
        es = small("es", [P, NH])
        den = small("den", [P, NH])
        rden = small("rden", [P, NH])
        V = small("V", [P, NT, 3])
        dsp = small("dsp", [P, 3])
        padr = small("padr", [P, 2])
        idt = small("idt", [P, 1])
        sst = small("sst", [P, 2, 8])
        stdt = small("stdt", [P, 2, 8])
        rinvt = small("rinvt", [P, 2, 8])
        q = small("q", [P, 4, 2])
        unit = small("unit", [P, 2])
        rowf = small("rowf", [P, 1])
        rcol = small("rcol", [P, NT])
        islice = at("islice", [P, P], F32, R2 + 38400)
        iug = small("iug", [P, 1], U32)
        ius = small("ius", [P, 1], U32)
        tri = at("tri", [P, P], F32, RC + 512)
        ones = at("ones", [P, P], F32, RC + 1024)
        code = at("code", [P, 3], F32, RC + 2176)
        io16 = at("io16", [P, MAXOVER], F32, RC + 2208)
        io32 = at("io32", [P, NEXP], F32, RC + 2272)
        one2 = small("one2", [2, P], F32R)
        one2f = small("one2f", [2, P])
        assert off <= 212800, off

        ps = nc.alloc_psum_tensor("ps", [P, 8, 512], F32)

        def slot2(s):
            return ps[:, 2 * s:2 * s + 2, :].rearrange("p b n -> p (b n)")

        m_dram = nc.dram_tensor("m_rows", (ROWS_DUMP, D), F32, kind="Internal").ap()
        h_dram = nc.dram_tensor("h_rows", (ROWS_DUMP, D), F32, kind="Internal").ap()
        bs_dram = nc.dram_tensor("bias_parts", (NEXP, 2, 3 * D), F32, kind="Internal").ap()

        landed = [sem(f"landed{s}") for s in range(RAW)]
        rounded = sem("rounded")
        split_done = sem("split_done")
        tiles_done = sem("tiles_done")
        c_in = sem("c_in")
        x_in = [sem(f"x_in{i}") for i in range(NT)]
        g_in = sem("g_in")
        br_in = sem("br_in")
        ck_in = sem("ck_in")
        vc_in = sem("vc_in")
        st_in = sem("st_in")
        b_rnd = sem("b_rnd")
        b_spl = sem("b_spl")
        b_out = sem("b_out")
        ss_done = sem("ss_done")
        std_done = sem("std_done")
        rinv_done = sem("rinv_done")
        xn_done = sem("xn_done")
        tr_done = sem("tr_done")
        th_done = sem("th_done")
        tl_done = sem("tl_done")
        pre_pe = sem("pre_pe")
        pre_act = sem("pre_act")
        pre_dve = sem("pre_dve")
        zev_act = sem("zev_act")
        zev_dve = sem("zev_dve")
        zero_done = sem("zero_done")
        conv_step = sem("conv_step")
        yc_h = sem("yc_h")
        yc_l = sem("yc_l")
        cst_done = sem("cst_done")
        cst_tr = sem("cst_tr")
        crow_done = sem("crow_done")
        at_sc = sem("at_sc")
        at_dv = sem("at_dv")
        at_ex = sem("at_ex")
        at_tr = sem("at_tr")
        at_ea = sem("at_ea")
        at_ed = sem("at_ed")
        at_pv = sem("at_pv")
        at_yh = sem("at_yh")
        at_yl = sem("at_yl")
        q_low = sem("q_low")
        k_high = sem("k_high")
        k_low = sem("k_low")
        qbd_done = sem("qbd_done")
        kv_out = sem("kv_out")
        kv_cp = sem("kv_cp")
        conv_out = sem("conv_out")
        sig_g = sem("sig_g")
        mg_step = sem("mg_step")
        mg_h = sem("mg_h")
        mg_l = sem("mg_l")
        xr_in = sem("xr_in")
        wo_ev = sem("wo_ev")
        r_in = sem("r_in")
        rc_in = sem("rc_in")
        m_done = sem("m_done")
        mtr = sem("mtr")
        mtr_ev = sem("mtr_ev")
        lg_mm = sem("lg_mm")
        r_step = sem("r_step")
        r_exp = sem("r_exp")
        rk_mm = sem("rk_mm")
        tab_done = sem("tab_done")
        rows_out = sem("rows_out")
        zrow_done = sem("zrow_done")
        pool_set = sem("pool_set")
        q_zero = sem("q_zero")
        io_in = sem("io_in")
        bup_in = sem("bup_in")
        bdn_in = sem("bdn_in")
        sel_step = sem("sel_step")
        rv_done = sem("rv_done")
        sel0 = sem("sel0")
        disp_mm = sem("disp_mm")
        disp_cp = sem("disp_cp")
        pq = sem("pq")
        gathered = sem("gathered")
        tx_done = sem("tx_done")
        xh_done = sem("xh_done")
        xl_done = sem("xl_done")
        gl_done = sem("gl_done")
        sig_done = sem("sig_done")
        u_done = sem("u_done")
        act_rows = sem("act_rows")
        ta_done = sem("ta_done")
        ah_done = sem("ah_done")
        al_done = sem("al_done")
        y_done = sem("y_done")
        scattered = sem("scattered")
        hb_in = [sem(f"hb_in{i}") for i in range(NT)]
        p_in = sem("p_in")
        gf_in = sem("gf_in")
        pp_mm = sem("pp_mm")
        pp_ev = sem("pp_ev")
        ss2 = sem("ss2")
        std2 = sem("std2")
        rinv2 = sem("rinv2")
        nrow = sem("nrow")
        ntr = sem("ntr")
        nhi = sem("nhi")
        nlo = sem("nlo")
        g_mm = sem("g_mm")
        g_sig = sem("g_sig")
        g_mul = sem("g_mul")
        g_add = sem("g_add")
        o_done = sem("o_done")
        out_done = sem("out_done")

        block = ctx.enter_context(nc.Block())

        def mix_uses(c):
            return c // RAW_MIX + 1

        used = [7, 6, 6, 6, 0, 0]

        def pro_slot(m):
            return (m + 4) % RAW

        def pro_use(m):
            s = pro_slot(m)
            return used[s] + 1 + (1 if m >= 6 else 0)

        used_body = [used[s] + (2 if s >= 4 else 1) for s in range(RAW)]

        @block.sync
        def _(sp):
            for i in range(NT):
                src = A["x_prompt"][0, P * i:P * i + P] if i < 4 else A["x_sample"].rearrange("n t d -> (n t) d")
                sp.dma_start(xin[0:ROWS[i], i, :], src).then_inc(x_in[i], 16)
                if i == 0:
                    sp.dma_start(gmix[:], A["g_mix"].broadcast_to([P, D])).then_inc(g_in, 16)
                    sp.dma_start(ident[:], A["c_ident"]).then_inc(g_in, 16)
                if i == 3:
                    sp.dma_start(raw[0][:], A["w_mix"][0]).then_inc(landed[0], 16)
            for c in range(1, RAW_MIX):
                sp.dma_start(raw[c][:], A["w_mix"][c]).then_inc(landed[c], 16)
            for t, n in ((negd, "c_negd"), (biass, "c_biass"), (sinks_s, "sink_rows"),
                         (cwT, "conv_cols"), (padr, "c_pad"), (V, "c_tok")):
                sp.dma_start(t[:], A[n]).then_inc(c_in, 16)
            sp.dma_start(sinkb[:], A["sinks"].broadcast_to([P, NH])).then_inc(c_in, 16)
            sp.dma_start(brow[:, 0:2 * FF], A["b_up"][0]).then_inc(br_in, 16)
            sp.dma_start(brow[:, 2 * FF:], A["b_down"][0]).then_inc(br_in, 16)
            sp.dma_start(ckrow[:], A["cache_k"][0].rearrange("n w g d -> w n (g d)")).then_inc(ck_in, 16)
            sp.dma_start(vc[:], A["cache_v"][0].rearrange("n w g d -> w n (g d)")).then_inc(vc_in, 16)
            sp.dma_start(strow[:], A["state_conv"][0].rearrange("n j c -> (n j) c")).then_inc(st_in, 16)
            for src, dst in (("cache_k", "k_sample"), ("cache_v", "v_sample")):
                sp.dma_start(O[dst][0][:, 0:WIN - TDEC].rearrange("n w g d -> n (w g d)"),
                             A[src][0][:, TDEC:].rearrange("n w g d -> n (w g d)")).then_inc(kv_cp, 16)
            sp.wait_ge(b_spl, 1)
            sp.dma_start(bs_dram[:, 0, :], bhi[:].bitcast(F32)).then_inc(b_out, 16)
            sp.dma_start(bs_dram[:, 1, :], blo[:].bitcast(F32)).then_inc(b_out, 16)
            kv_stored = False
            for c in range(RAW_MIX, NM):
                sp.wait_ge(split_done, c - RAW_MIX + 1)
                sp.dma_start(raw[c % RAW_MIX][:], A["w_mix"][c]).then_inc(landed[c % RAW_MIX], 16)
                if c == Z_CHUNKS + 4:
                    sp.wait_ge(crow_done, 1)
                    sp.dma_start(O["conv_prompt"][0, 0], crow[0:2, :]).then_inc(conv_out, 16)
                    sp.dma_start(O["conv_sample"][0].rearrange("n j c -> (n j) c"), crow[2:18, :]).then_inc(conv_out, 16)
                if c == 6:
                    sp.wait_ge(pre_act, 3)
                    sp.dma_start(O["k_prompt"][0, 0].rearrange("w g d -> w (g d)"), krow[:, 0, :]).then_inc(kv_out, 16)
                    sp.dma_start(O["v_prompt"][0, 0].rearrange("w g d -> w (g d)"), vrow[:, 3, :]).then_inc(kv_out, 16)
                    for n in range(NSEQ):
                        sp.dma_start(O["k_sample"][0, n, WIN - TDEC:].rearrange("w g d -> w (g d)"),
                                     krow[TDEC * n:TDEC * n + TDEC, 1, :]).then_inc(kv_out, 16)
                        sp.dma_start(O["v_sample"][0, n, WIN - TDEC:].rearrange("w g d -> w (g d)"),
                                     vrow[TDEC * n:TDEC * n + TDEC, 4, :]).then_inc(kv_out, 16)
            sp.wait_ge(tiles_done, tiles_after(Z_CHUNKS + BR_CHUNKS - 2))
            sp.dma_start(hrow[:, 0:4, :], A["x_prompt"][0].rearrange("(i p) d -> p i d", p=P)).then_inc(xr_in, 16)
            sp.dma_start(hrow[0:TS, 4, :], A["x_sample"].rearrange("n t d -> (n t) d")).then_inc(xr_in, 16)
            sp.wait_ge(tiles_done, tiles_after(Z_CHUNKS + BR_CHUNKS - 1))
            sp.dma_start(gffn[:], A["g_ffn"].broadcast_to([P, D])).then_inc(r_in, 16)
            sp.dma_start(wr[:], A["w_router"][0].rearrange("(k p) e -> p k e", p=P)).then_inc(r_in, 16)
            sp.dma_start(brt[:], A["b_router"].broadcast_to([P, NEXP])).then_inc(r_in, 16)
            for t, n in ((tri, "c_tri"), (ones, "c_ones"), (code, "c_code"), (io16, "c_io16"), (io32, "c_io32")):
                sp.dma_start(t[:], A[n]).then_inc(rc_in, 16)
            w_up = A["w_up"][0].rearrange("e (k p) n -> e k p n", p=P)
            w_dn = A["w_down"][0].rearrange("e (c j p) n -> e c p j n", j=2, p=P)
            for m in (3, 4, 5, 2):
                s = pro_slot(m)
                sp.wait_ge(split_done, {0: 24, 1: 21, 2: 22, 3: 23}[s] + 1)
                sp.dma_start(raw[s][:], w_up[0, m]).then_inc(landed[s], 16)
            sp.dma_start(h_dram[T:ROWS_DUMP], A["c_zero"]).then_inc(rows_out, 16)
            sp.dma_start(m_dram[T:ROWS_DUMP], A["c_zero"]).then_inc(rows_out, 16)
            for i in range(NT):
                if i == NT - 1:
                    sp.wait_ge(tiles_done, TB)
                    for m in range(2):
                        sp.dma_start(raw[pro_slot(m)][:], w_up[0, m]).then_inc(landed[pro_slot(m)], 16)
                    sp.dma_start(iota[:], A["c_iota"]).then_inc(io_in, 16)
                rows = slice(P * i, P * i + ROWS[i])
                sp.wait_ge(wo_ev, i + 1)
                sp.dma_start(h_dram[rows], hrow[0:ROWS[i], i, :]).then_inc(rows_out, 16)
                sp.wait_ge(m_done, i + 1)
                sp.dma_start(m_dram[rows], mrow[0:ROWS[i], i, :]).then_inc(rows_out, 16)
            sp.wait_ge(b_out, 32)
            sp.dma_start(bup[:].bitcast(F32), bs_dram[0, :, 0:2 * FF]).then_inc(bup_in, 16)
            for m in (6, 7):
                sp.wait_ge(split_done, NM + m - RAW + 1)
                sp.dma_start(raw[pro_slot(m)][:], w_up[0, m]).then_inc(landed[pro_slot(m)], 16)
            sp.wait_ge(tab_done, 1)
            end = sp.value_load(tabN[0:1, 0:1], min_val=NEXP, max_val=NEXP + MAXOVER)
            nb = sp.value_load(tabN[0:1, 1:2], min_val=NEXP - PEEL, max_val=NEXP + MAXOVER - PEEL) + PEEL

            def body(i, first):
                e_cur = sp.value_load(tabE[0:1, bass.ds(i, 1)], min_val=0, max_val=NEXP - 1)
                e_prev = sp.value_load(tabE[0:1, bass.ds(i - 1, 1)], min_val=0, max_val=NEXP - 1)
                sp.wait_ge(tiles_done, TB + 1 if first else TB + 12 * i - 15)
                sp.dma_start(bup[:].bitcast(F32), bs_dram[bass.ds(e_cur, 1), :, 0:2 * FF].rearrange("e j n -> (e j) n"))\
                  .then_inc(bup_in, 16)
                for l in range(BLK):
                    if l == UPC:
                        if not first:
                            sp.wait_ge(tiles_done, TB + 12 * i - 7)
                        sp.dma_start(bdn[:].bitcast(F32), bs_dram[bass.ds(e_prev, 1), :, 2 * FF:].rearrange("e j n -> (e j) n"))\
                          .then_inc(bdn_in, 16)
                    sp.wait_ge(split_done, NM + 12 * i - 4 + l - RAW + 1)
                    if l < UPC:
                        src = w_up[bass.ds(e_cur, 1), l].rearrange("e p n -> (e p) n")
                    else:
                        src = w_dn[bass.ds(e_prev, 1), l - UPC].rearrange("e p j n -> (e p) j n")
                    dst = raw[l % RAW][:] if l < UPC else raw[l % RAW][:].rearrange("p (j n) -> p j n", j=2)
                    sp.dma_start(dst, src).then_inc(landed[l % RAW], 16)

            body(1, True)
            body(2, False)
            with sp.Fori(PEEL, end) as i:
                body(i, False)
            e_prev = sp.value_load(tabE[0:1, bass.ds(nb - 1, 1)], min_val=0, max_val=NEXP - 1)
            sp.wait_ge(rv_done, nb + 1)
            sp.dma_start(prow[:, 0:4, :], A["p_prompt"][0, 0].rearrange("(i p) d -> p i d", p=P)).then_inc(p_in, 16)
            sp.dma_start(prow[0:TS, 4, :], A["p_sample"][0].rearrange("n t d -> (n t) d")).then_inc(p_in, 16)
            sp.wait_ge(tiles_done, TB + 12 * nb - 7)
            sp.dma_start(bdn[:].bitcast(F32), bs_dram[bass.ds(e_prev, 1), :, 2 * FF:].rearrange("e j n -> (e j) n")).then_inc(bdn_in, 16)
            for l in range(DNC):
                sp.wait_ge(split_done, NM + 12 * nb - 4 + l - RAW + 1)
                sp.dma_start(raw[l % RAW][:].rearrange("p (j n) -> p j n", j=2),
                             w_dn[bass.ds(e_prev, 1), l].rearrange("e p j n -> (e p) j n")).then_inc(landed[l % RAW], 16)
            for g in range(PLE_CHUNKS):
                s = (4 + g) % RAW
                sp.wait_ge(split_done, NM + 12 * nb + g - RAW + 1)
                sp.dma_start(raw[s][:], A["w_ple_chunks"][g]).then_inc(landed[s], 16)
            sp.dma_start(gple[:], A["g_ple"].broadcast_to([P, D])).then_inc(gf_in, 16)
            sp.wait_ge(tr_done, NT + 2)
            sp.dma_start(gfin[:], A["g_final"].rearrange("(a d) -> a d", a=1).broadcast_to([P, D])).then_inc(gf_in, 16)
            sp.wait_ge(scattered, 16 * nb)
            for i in range(NT):
                src = h_dram[P * i:P * i + ROWS[i]]
                sp.dma_start(hrow[0:ROWS[i], i, :], src).then_inc(hb_in[i], 16)
            for i in range(NT):
                sp.wait_ge(o_done, i + 1)
                if i < 4:
                    sp.dma_start(O["y_prompt"][0, P * i:P * i + P], hrow[:, i, :]).then_inc(out_done, 16)
                else:
                    sp.dma_start(O["y_sample"].rearrange("n t d -> (n t) d"), hrow[0:TS, 4, :]).then_inc(out_done, 16)
            sp.wait_ge(out_done, 16 * NT)
            sp.wait_ge(kv_out, 16 * 18)
            sp.wait_ge(conv_out, 32)
            sp.wait_ge(kv_cp, 32)

        @block.gpsimd
        def _(pool):
            nc.gpsimd.memset(upP[:, :, 0:2], 0.0).then_inc(zero_done, 1)
            nc.gpsimd.memset(qbd[:], 0.0).then_inc(zero_done, 1)
            nc.gpsimd.memset(one2f[:], 1.0).then_inc(zero_done, 1)
            nc.gpsimd.memset(q[:], 0.0).then_inc(q_zero, 1)
            nc.gpsimd.memset(unit[:], 1.0).then_inc(q_zero, 1)
            pool.wait_ge(q_zero, 2)
            pool.wait_ge(io_in, 16)
            pool.wait_ge(c_in, 16 * 7)

            def select(b, e, base):
                nc.gpsimd.tensor_copy(rcol[:].unsqueeze(2), rankm[:, :, bass.ds(e, 1)]).then_inc(sel_step, 1)
                nc.gpsimd.tensor_copy(islice[:], iota[:, bass.ds(base, P)]).then_inc(sel_step, 1)
                nc.gpsimd.tensor_copy(V[:, :, 2:3], gate[:, :, bass.ds(e, 1)]).then_inc(sel_step, 1)
                pool.drain()
                for t in range(NT):
                    ins = nc.gpsimd.tensor_scalar(Rsel[:, t, :], islice[:], rcol[:, t:t + 1], None, ALU.is_equal)
                ins.then_inc(rv_done, 1)

            def select_block(b):
                e = pool.value_load(tabE[0:1, bass.ds(b, 1)], min_val=0, max_val=NEXP - 1)
                base = pool.value_load(tabB[0:1, bass.ds(b, 1)], min_val=0, max_val=4 * P)
                select(b, e, base)

            def dispatch(b):
                pool.wait_ge(disp_cp, b + 1)
                nc.gpsimd.tensor_tensor(q[:, 3, :], q[:, 2, :], unit[:], ALU.mult).then_inc(pq, 1)
                pool.drain()
                nc.gpsimd.tensor_copy(q[:, 2, :], q[:, 1, :]).then_inc(pq, 1)
                pool.drain()
                nc.gpsimd.tensor_copy(q[:, 1, :], q[:, 0, :]).then_inc(pq, 1)
                nc.gpsimd.tensor_scalar(idt[:], dsp[:, 1:2], padr[:, 0:1], padr[:, 1:2], ALU.mult, ALU.add).then_inc(pq, 1)
                pool.drain()
                nc.gpsimd.tensor_tensor(q[:, 0, 0:1], idt[:], dsp[:, 0:1], ALU.add).then_inc(pq, 1)
                nc.gpsimd.tensor_copy(q[:, 0, 1:2], dsp[:, 2:3]).then_inc(pq, 1)
                pool.drain()
                nc.gpsimd.tensor_copy(iug[:], q[:, 0, 0:1]).then_inc(pq, 1)
                pool.drain()
                nc.gpsimd.indirect_dma_start(xg[:], None, m_dram, bass.IndirectOffsetOnAxis(ap=iug[:, 0:1], axis=0),
                                             bounds_check=ROWS_DUMP - 1).then_inc(gathered, 16)

            def scatter(i, col):
                pool.wait_ge(y_done, i + 1)
                nc.gpsimd.tensor_tensor(rowf[:], q[:, col, 0:1], unit[:, 0:1], ALU.mult).then_inc(pool_set, 1)
                pool.drain()
                nc.gpsimd.tensor_copy(ius[:], rowf[:]).then_inc(pool_set, 1)
                pool.drain()
                nc.gpsimd.indirect_dma_start(h_dram, bass.IndirectOffsetOnAxis(ap=ius[:, 0:1], axis=0), yrow[:], None,
                                             bounds_check=ROWS_DUMP - 1, compute_op=ALU.add).then_inc(scattered, 16)

            pool.wait_ge(rows_out, 16 * (2 + 2 * NT))
            dispatch(0)
            pool.wait_ge(tab_done, 1)
            end = pool.value_load(tabN[0:1, 0:1], min_val=NEXP, max_val=NEXP + MAXOVER)
            nb = pool.value_load(tabN[0:1, 1:2], min_val=NEXP - PEEL, max_val=NEXP + MAXOVER - PEEL) + PEEL
            select_block(1)
            pool.wait_ge(tx_done, 1)
            dispatch(1)
            select_block(2)
            pool.wait_ge(tx_done, 2)
            dispatch(2)
            select_block(3)
            pool.wait_ge(tx_done, 3)
            dispatch(3)
            select_block(4)
            scatter(0, 3)
            with pool.Fori(PEEL, end) as i:
                pool.wait_ge(tx_done, i + 1)
                pool.wait_ge(y_done, i - 2)
                dispatch(i + 1)
                select_block(i + 2)
                pool.wait_ge(scattered, 16 * i - 32)
                scatter(i - 2, 3)
            for back, col in ((2, 2), (1, 1)):
                pool.wait_ge(scattered, 16 * nb - 16 * back)
                scatter(nb - back, col)
            pool.wait_ge(scattered, 16 * nb)

        @block.scalar
        def _(act):
            def round_chunk(s, slot, land):
                act.wait_ge(landed[s], land)
                nc.scalar.activation(wh[slot][:], raw[s][:], ACT.Copy).then_inc(rounded, 1)

            def round_mix(c):
                if c >= SPL_MIX:
                    act.wait_ge(tiles_done, tiles_after(c - SPL_MIX))
                round_chunk(c % RAW_MIX, c % SPL_MIX, 16 * mix_uses(c))

            def round_wo(g):
                c = Z_CHUNKS + BR_CHUNKS + g
                if g == 0:
                    act.wait_ge(tiles_done, tiles_after(c - SPL_MIX))
                elif g == 1:
                    act.wait_ge(conv_out, 32)
                elif g == 2:
                    act.wait_ge(tiles_done, tiles_after(c - SPL_MIX - 1))
                else:
                    act.wait_ge(mg_l, KT)
                act.wait_ge(landed[c % RAW_MIX], 16 * mix_uses(c))
                nc.scalar.activation(wo_h[g][:], raw[c % RAW_MIX][:], ACT.Copy).then_inc(rounded, 1)

            def x_stat(i):
                r = ROWS[i]
                act.wait_ge(x_in[i], 16)
                if i:
                    act.wait_ge(ss_done, i)
                nc.scalar.activation(slot2(3)[0:r, :], xin[0:r, i, :], ACT.Square, accum_out=ss[0:r, i:i + 1])\
                  .then_inc(ss_done, 1)
                act.wait_ge(ss_done, i + 1)
                nc.scalar.activation(std[0:r, i:i + 1], ss[0:r, i:i + 1], ACT.Sqrt, scale=1.0 / D, bias=epsb[0:r, 0:1])\
                  .then_inc(std_done, 1)

            def x_high(i):
                act.wait_ge(tr_done, i + 1)
                r = ROWS[i]
                nc.scalar.activation(aTh[:, :, P * i:P * i + r],
                                     slot2(i % 3)[:, 0:KT * r].rearrange("p (k n) -> p k n", k=KT), ACT.Copy)\
                  .then_inc(th_done, 1)

            act.wait_ge(pre_dve, 1)
            x_stat(0)
            for i in range(1, NT):
                x_stat(i)
                x_high(i - 1)
            round_mix(0)
            x_high(NT - 1)
            round_mix(1)
            act.wait_ge(br_in, 32)
            nc.scalar.activation(bhi[:], brow[:], ACT.Copy).then_inc(b_rnd, 1)
            act.wait_ge(zero_done, 3)
            nc.scalar.activation(one2[:], one2f[:], ACT.Copy).then_inc(b_rnd, 1)
            def z_copy(n):
                act.wait_ge(tiles_done, n + 1)
                src = slot2(n % 2).rearrange("p (b n) -> p b n", b=2)[:, :, 0:HALF]
                if n < 2:
                    ins = nc.scalar.activation(kvT[:, n, :].rearrange("p (b n) -> p b n", b=2), src, ACT.Copy)
                elif n < 6:
                    nc.scalar.activation(qTh[:, n - 2, 0:HALF], src[:, 0, :], ACT.Copy)
                    nc.scalar.activation(qTh[:, n - 2, HALF:], src[:, 1, 0:SEQ - HALF], ACT.Copy)
                    ins = nc.scalar.activation(qS[:, n - 2, :], src[:, 1, SEQ - HALF:HALF], ACT.Copy)
                else:
                    c = n - 6
                    nc.scalar.activation(upP[:, c, 2:2 + HALF], src[:, 0, :], ACT.Copy)
                    nc.scalar.activation(upP[:, c, 2 + HALF:2 + SEQ], src[:, 1, 0:SEQ - HALF], ACT.Copy)
                    ins = nc.scalar.activation(upS[:, c, :, 2:6],
                                               src[:, 1, SEQ - HALF:HALF].rearrange("p (n t) -> p n t", t=TDEC), ACT.Copy)
                ins.then_inc(zev_act, 1)

            def exps(n):
                lo = WIN if n == 0 else 0
                act.wait_ge(at_dv, 6 * n + 5)
                for h in range(NH):
                    nc.scalar.activation(S[:, h, lo:], S[:, h, lo:], ACT.Exp, bias=negm[:, h:h + 1], scale=SCALE,
                                         accum_out=den[:, h:h + 1])
                nc.scalar.activation(es[:], esi[:], ACT.Exp).then_inc(at_ex, 1)

            def probs(n):
                act.wait_ge(at_tr, n + 1)
                lo = 1 if n == 0 else 0
                nc.scalar.activation(PT[:, 0:8, :].rearrange("p (h k) q -> p h k q", k=2)[:, :, lo:, :],
                                     ps[:, 4:6, :].rearrange("p b (h k q) -> p (b h) k q", k=2, q=P)[:, :, lo:, :],
                                     ACT.Copy).then_inc(at_ea, 1)

            def mixed(n):
                act.wait_ge(at_pv, n + 1)
                nc.scalar.activation(yTh[:, CT:2 * CT, P * n:P * n + P],
                                     ps[:, 4, :].rearrange("p (j q) -> p j q", j=CT), ACT.Copy).then_inc(at_yh, 1)

            for c in range(3):
                z_copy(2 * c)
                z_copy(2 * c + 1)
                if c == 0:
                    act.wait_ge(zev_act, 1)
                    nc.scalar.activation(kTh[:], kvT[:, 0, 0:SEQ], ACT.Copy).then_inc(k_high, 1)
                    act.wait_ge(pre_pe, 2)
                    act.wait_ge(b_out, 32)
                    nc.scalar.activation(ksT[:].rearrange("p n w -> p (n w)"),
                                         ps[:, 5:7, :].rearrange("p b n -> p (b n)"), ACT.Copy).then_inc(pre_act, 1)
                if c == 1:
                    act.wait_ge(pre_pe, 3)
                    nc.scalar.activation(vrow[:, 0:4, :].rearrange("p i n -> p (i n)"), ps[:, 4, :], ACT.Copy)
                    nc.scalar.activation(vrow[0:TS, 4, :], ps[0:TS, 5, 0:P], ACT.Copy).then_inc(pre_act, 1)
                    nc.scalar.activation(krow[:, 0, :], ps[:, 5, P:2 * P], ACT.Copy)
                    nc.scalar.activation(krow[0:TS, 1, :], ps[0:TS, 5, 2 * P:3 * P], ACT.Copy).then_inc(pre_act, 1)
                round_mix(c + 2)
            exps(0)
            z_copy(6)
            z_copy(7)
            round_mix(5)
            probs(0)
            z_copy(8)
            mixed(0)
            exps(1)
            z_copy(9)
            round_mix(6)
            probs(1)
            round_mix(7)
            mixed(1)
            exps(2)
            round_mix(8)
            probs(2)
            mixed(2)
            exps(3)
            round_mix(9)
            probs(3)
            round_mix(10)
            mixed(3)
            for c in range(CT):
                act.wait_ge(zev_dve, CT + c + 1)
                nc.scalar.activation(yTh[:, c, :], cv[:, c, :], ACT.Copy).then_inc(yc_h, 1)
            act.wait_ge(at_dv, 6 * 4 + 4)
            for a in range(2):
                nc.scalar.activation(Ss[:, a, :], Ss[:, a, :], ACT.Exp, bias=negm[:, a:a + 1], scale=SCALE,
                                     accum_out=den[:, a:a + 1])
                nc.scalar.activation(es[:, a:a + 1], negm[:, a:a + 1], ACT.Exp, bias=sinks_s[:, 0:1]).then_inc(at_ex, 1)
            act.wait_ge(at_tr, 5)
            nc.scalar.activation(PsT[:].rearrange("p a n -> p (a n)"), ps[:, 5, 0:2 * P], ACT.Copy)
            nc.scalar.activation(PsN[:].rearrange("p a n -> p (a n)"), ps[0:TS, 6, 0:2 * P], ACT.Copy).then_inc(at_ea, 1)
            act.wait_ge(at_pv, 5)
            nc.scalar.activation(yTh[:, CT:2 * CT, SEQ:T].rearrange("p j (n t) -> p j n t", t=TDEC),
                                 ps[:, 7, 0:P].rearrange("p (n j t) -> p j n t", n=NSEQ, t=TDEC), ACT.Copy).then_inc(at_yh, 1)
            act.wait_ge(cst_tr, 1)
            nc.scalar.activation(crow[:], ps[0:18, 4, :], ACT.Copy).then_inc(crow_done, 1)
            for dp in range(PAIRS):
                c = Z_CHUNKS + 3 * dp
                for r in range(2):
                    for u in range(2):
                        act.wait_ge(tiles_done, tiles_after(c + r - 1) + u + 1)
                        if dp > 0:
                            act.wait_ge(mg_l, 2 * dp - 1 + u)
                        else:
                            act.wait_ge(at_ed, 4)
                            act.wait_ge(at_pv, 5)
                        src = slot2(2 * r + u).rearrange("p (b n) -> p b n", b=2)[:, :, 0:HALF]
                        nc.scalar.activation(sg[:, u, r, :].rearrange("p (b n) -> p b n", b=2), src, ACT.Sigmoid)\
                          .then_inc(sig_g, 1)
                    if dp == PAIRS - 1 and r == 1:
                        round_wo(0)
                        round_wo(1)
                    else:
                        round_mix(c + r + 2)
                for u in range(2):
                    d = 2 * dp + u
                    act.wait_ge(mg_step, 3 * (d + 1))
                    if d == 0:
                        act.wait_ge(kv_out, 16 * 18)
                    nc.scalar.activation(mTh[:, d, :], sg[:, u, 0, :], ACT.Copy).then_inc(mg_h, 1)
                    if u == 0 and dp < PAIRS - 1:
                        round_mix(c + 4)
                    elif u == 0:
                        round_wo(2)
            round_wo(3)

            def moe_stat(i):
                r = ROWS[i]
                act.wait_ge(wo_ev, i + 1)
                nc.scalar.activation(mrow[0:r, i, :], hrow[0:r, i, :], ACT.Square, accum_out=ss[0:r, i:i + 1])\
                  .then_inc(ss_done, 1)
                act.wait_ge(ss_done, NT + i + 1)
                nc.scalar.activation(std[0:r, i:i + 1], ss[0:r, i:i + 1], ACT.Sqrt, scale=1.0 / D, bias=epsb[0:r, 0:1])\
                  .then_inc(std_done, 1)

            def m_copy(i):
                act.wait_ge(mtr, i + 1)
                if i >= 2:
                    act.wait_ge(lg_mm, i - 1)
                nc.scalar.activation(mTf[:, i % 2, 0:KT * ROWS[i]], slot2(2)[:, 0:KT * ROWS[i]], ACT.Copy).then_inc(mtr_ev, 1)

            moe_stat(0)
            for i in range(1, NT):
                moe_stat(i)
                m_copy(i - 1)
            m_copy(NT - 1)
            act.wait_ge(r_step, R0S + ROUT * (NT - 1) + 3)
            nc.scalar.activation(ev[:], ev[:], ACT.Exp).then_inc(r_exp, 1)

            def round_pro(m):
                if m == 0:
                    act.wait_ge(tiles_done, TB)
                elif m >= 3:
                    act.wait_ge(tiles_done, TB + m - 2)
                round_chunk(pro_slot(m), (m + 1) % SPL, 16 * pro_use(m))

            def round_body(i, l):
                act.wait_ge(tiles_done, TB + 12 * i - 4 + l - SPL + 1)
                round_chunk(l % RAW, l % SPL, 32 * i + 16 * (used_body[l % RAW] + l // RAW - 1))

            def disp_copy(b):
                act.wait_ge(disp_mm, b + 1)
                nc.scalar.activation(dsp[:], ps[:, 6, 0:3], ACT.Copy).then_inc(disp_cp, 1)

            def xh_copy(b, up_done):
                act.wait_ge(tx_done, b + 1)
                if up_done is not None:
                    act.wait_ge(tiles_done, up_done)
                nc.scalar.activation(xTh[:].rearrange("p k n -> p (k n)"), slot2(3), ACT.Copy).then_inc(xh_done, 1)

            def sigm(i, hf):
                act.wait_ge(gl_done, 2 * i + hf + 1)
                nc.scalar.activation(sgm[:, 512 * hf:512 * hf + 512], gl[:, 0, 512 * hf:512 * hf + 512], ACT.Sigmoid,
                                     scale=ALPHA).then_inc(sig_done, 1)

            def ah_copy(i):
                act.wait_ge(ta_done, i + 1)
                nc.scalar.activation(acTh[:].rearrange("p k n -> p (k n)"), slot2(3), ACT.Copy).then_inc(ah_done, 1)

            def y_copy(gcol, chunk_done):
                act.wait_ge(tiles_done, chunk_done)
                nc.scalar.activation(yrow[:], slot2(2), ACT.Copy, scale=gcol).then_inc(y_done, 1)

            round_pro(0)
            round_pro(1)
            round_pro(2)
            disp_copy(0)
            xh_copy(0, None)
            round_pro(3)
            disp_copy(1)
            for m in range(4, 8):
                round_pro(m)
            round_body(1, 0)
            round_body(1, 1)
            xh_copy(1, TB + 8)
            round_body(1, 2)
            sigm(0, 0)

            def body(i, first):
                for l in range(BLK):
                    if not (first and l < 3):
                        round_body(i, l)
                    if l == (2 if first else 0):
                        sigm(i - 1, 1)
                    if l == 2:
                        disp_copy(i + 1)
                        if not first:
                            act.wait_ge(pq, 7 * i + 8)
                            if not (isinstance(i, int) and i == 2):
                                act.wait_ge(scattered, 16 * i - 32)
                            y_copy(q[:, 3, 1:2], TB + 12 * i - 4)
                    if l == 6:
                        ah_copy(i - 1)
                    if l == 10:
                        xh_copy(i + 1, TB + 12 * i + 4)
                sigm(i, 0)

            body(1, True)
            body(2, False)
            end = act.value_load(tabN[0:1, 0:1], min_val=NEXP, max_val=NEXP + MAXOVER)
            nb = act.value_load(tabN[0:1, 1:2], min_val=NEXP - PEEL, max_val=NEXP + MAXOVER - PEEL) + PEEL
            with act.Fori(PEEL, end) as i:
                body(i, False)
            sigm(nb - 1, 1)
            round_body(nb, 0)
            act.wait_ge(pq, 7 * nb + 7)
            act.wait_ge(scattered, 16 * nb - 32)
            y_copy(q[:, 2, 1:2], TB + 12 * nb - 4)
            for k in range(2):
                act.wait_ge(tr_done, NT + k + 1)
                nc.scalar.activation(pTh[:, k, :], slot2(k)[:, 0:T], ACT.Copy).then_inc(th_done, 1)
            ah_copy(nb - 1)
            for l in range(1, DNC):
                round_body(nb, l)

            def round_ple(g, dst):
                slot = (4 + g) % RAW
                fills = used_body[slot] + (1 if slot < DNC else 0) + 1
                act.wait_ge(landed[slot], 32 * nb - 32 + 16 * fills)
                nc.scalar.activation(dst[:], raw[slot][:], ACT.Copy).then_inc(rounded, 1)

            act.wait_ge(tiles_done, TB + 12 * nb - 2)
            round_ple(0, wh[1])
            act.wait_ge(tiles_done, TB + 12 * nb - 1)
            round_ple(1, gate_h[0])
            act.wait_ge(scattered, 16 * nb - 16)
            y_copy(q[:, 1, 1:2], TB + 12 * nb)
            round_ple(2, gate_h[1])
            act.wait_ge(split_done, NM + 12 * nb + 1)
            round_ple(3, gate_h[2])

            def pp_copy(i):
                act.wait_ge(pp_mm, i + 1)
                nc.scalar.activation(pp[0:ROWS[i], i, :], slot2(PP_SLOT[i])[0:ROWS[i], :], ACT.Copy).then_inc(pp_ev, 1)

            def norm_stat(which, i):
                n, c = NORMS.index((which, i)), 0 if which == "in" else 1
                r = ROWS[i]
                if n:
                    act.wait_ge(ss2, n)
                if which == "in":
                    act.wait_ge(hb_in[i], 16)
                else:
                    act.wait_ge(g_add, i + 1)
                nc.scalar.activation(slot2(3)[0:r, :], hrow[0:r, i, :], ACT.Square, accum_out=sst[0:r, c, i:i + 1])\
                  .then_inc(ss2, 1)
                act.wait_ge(ss2, n + 1)
                nc.scalar.activation(stdt[0:r, c, i:i + 1], sst[0:r, c, i:i + 1], ACT.Sqrt, scale=1.0 / D,
                                     bias=epsb[0:r, 0:1]).then_inc(std2, 1)

            def n_high(i):
                act.wait_ge(ntr, i + 1)
                r = ROWS[i]
                nc.scalar.activation(nTh[:, :, P * i:P * i + r],
                                     slot2(2)[:, 0:KT * r].rearrange("p (k n) -> p k n", k=KT), ACT.Copy).then_inc(nhi, 1)

            for i in range(3):
                pp_copy(i)
            act.wait_ge(pp_ev, 3)
            norm_stat("in", 0)
            pp_copy(3)
            norm_stat("in", 1)
            pp_copy(4)
            round_ple(4, gate_h[3])
            n_high(0)
            norm_stat("in", 2)
            n_high(1)
            for i in range(NT):
                act.wait_ge(g_mm, i + 1)
                nc.scalar.activation(xnb[0:ROWS[i], i % 3, :], slot2(i % 2)[0:ROWS[i], :], ACT.Sigmoid).then_inc(g_sig, 1)
                if i + 2 < NT:
                    n_high(i + 2)
                norm_stat("out", i)
                if i + 3 < NT:
                    norm_stat("in", i + 3)

        @block.vector
        def _(dve):
            def split(cnt, s, slot):
                dve.wait_ge(rounded, cnt)
                nc.vector.tensor_tensor(wl[slot][:], raw[s][:], wh[slot][:].bitcast(F32), ALU.subtract)\
                  .then_inc(split_done, 1)

            def split_mix(c):
                split(c + 1, c % RAW_MIX, c % SPL_MIX)

            def split_wo(g):
                c = Z_CHUNKS + BR_CHUNKS + g
                dve.wait_ge(rounded, c + 1)
                nc.vector.tensor_tensor(wo_l[g][:], raw[c % RAW_MIX][:], wo_h[g][:].bitcast(F32), ALU.subtract)\
                  .then_inc(split_done, 1)

            def x_rows(i):
                r = ROWS[i]
                dve.wait_ge(std_done, i + 1)
                nc.vector.reciprocal(rinv[0:r, i:i + 1], std[0:r, i:i + 1]).then_inc(rinv_done, 1)
                dve.wait_ge(rinv_done, i + 1)
                nc.vector.scalar_tensor_tensor(out=xin[0:r, i, :], in0=xin[0:r, i, :], scalar=rinv[0:r, i:i + 1],
                                               in1=gmix[0:r, :], op0=ALU.mult, op1=ALU.mult).then_inc(xn_done, 1)

            def x_low(i):
                dve.wait_ge(th_done, i + 1)
                tok = slice(P * i, P * i + ROWS[i])
                nc.vector.tensor_tensor(aTl[:, :, tok], slot2(i % 3)[:, 0:KT * ROWS[i]].rearrange("p (k n) -> p k n", k=KT),
                                        aTh[:, :, tok].bitcast(F32), ALU.subtract).then_inc(tl_done, 1)

            nc.vector.memset(epsb[:], EPS).then_inc(pre_dve, 1)
            dve.wait_ge(g_in, 32)
            x_rows(0)
            for i in range(1, NT):
                x_rows(i)
                x_low(i - 1)
            split_mix(0)
            x_low(NT - 1)
            split_mix(1)
            dve.wait_ge(b_rnd, 1)
            nc.vector.tensor_tensor(blo[:], brow[:], bhi[:].bitcast(F32), ALU.subtract).then_inc(b_spl, 1)
            dve.wait_ge(pre_pe, 1)
            nc.vector.tensor_copy(upS[:, :, :, 0:2], ps[:, 4, 0:64].rearrange("p (c n j) -> p c n j", c=CT, j=2))\
              .then_inc(pre_dve, 1)

            def soft_a(n):
                lo = WIN if n == 0 else 0
                dve.wait_ge(at_sc, n + 1)
                if n > 0:
                    dve.wait_ge(at_yl, n)
                else:
                    dve.wait_ge(b_out, 32)
                for h in range(NH):
                    ins = nc.vector.scalar_tensor_tensor(
                        out=S[:, h, lo:], in0=negd[:, lo:], scalar=SLOPE[h] / SCALE,
                        in1=ps[:, 4 + h // 2, 256 * (h % 2) + lo:256 * (h % 2) + 256], op0=ALU.mult, op1=ALU.add)
                ins.then_inc(at_dv, 1)
                dve.wait_ge(at_dv, 6 * n + 1)
                nc.vector.tensor_reduce(mx[:], S[:, :, lo:], AX_X, ALU.max).then_inc(at_dv, 1)
                dve.wait_ge(at_dv, 6 * n + 2)
                nc.vector.scalar_tensor_tensor(out=mm[:], in0=mx[:], scalar=SCALE, in1=sinkb[:], op0=ALU.mult, op1=ALU.max)\
                  .then_inc(at_dv, 1)
                dve.wait_ge(at_dv, 6 * n + 3)
                nc.vector.tensor_tensor(esi[:], sinkb[:], mm[:], ALU.subtract).then_inc(at_dv, 1)
                nc.vector.tensor_scalar(negm[:], mm[:], -1.0, None, ALU.mult).then_inc(at_dv, 1)

            def soft_b(n):
                lo = WIN if n == 0 else 0
                dve.wait_ge(at_ex, n + 1)
                nc.vector.tensor_tensor(den[:], den[:], es[:], ALU.add).then_inc(conv_step, 1)
                steps[0] += 1
                dve.wait_ge(conv_step, steps[0])
                nc.vector.reciprocal(rden[:], den[:]).then_inc(conv_step, 1)
                steps[0] += 1
                dve.wait_ge(conv_step, steps[0])
                for h in range(NH):
                    ins = nc.vector.tensor_scalar(S[:, h, lo:], S[:, h, lo:], rden[:, h:h + 1], None, ALU.mult)
                ins.then_inc(at_dv, 1)

            def probs(n):
                dve.wait_ge(at_tr, n + 1)
                lo = 1 if n == 0 else 0
                nc.vector.tensor_copy(PT[:, 8:16, :].rearrange("p (h k) q -> p h k q", k=2)[:, :, lo:, :],
                                      ps[:, 6:8, :].rearrange("p b (h k q) -> p (b h) k q", k=2, q=P)[:, :, lo:, :])\
                  .then_inc(at_ed, 1)

            def mixed(n):
                dve.wait_ge(at_yh, n + 1)
                nc.vector.tensor_tensor(yTl[:, CT:2 * CT, P * n:P * n + P],
                                        ps[:, 4, :].rearrange("p (j q) -> p j q", j=CT),
                                        yTh[:, CT:2 * CT, P * n:P * n + P].bitcast(F32), ALU.subtract).then_inc(at_yl, 1)

            steps, conv_done = [0], []

            def z_mult(n):
                dve.wait_ge(tiles_done, n + 1)
                src = slot2(n % 2).rearrange("p (b n) -> p b n", b=2)[:, :, 0:HALF]
                if n < 14:
                    c = n - 10
                    dve.wait_ge(zev_act, 6 + c + 1)
                    nc.vector.tensor_tensor(upP[:, c, 2:2 + HALF], src[:, 0, :], upP[:, c, 2:2 + HALF], ALU.mult)
                    nc.vector.tensor_tensor(upP[:, c, 2 + HALF:], src[:, 1, 0:SEQ - HALF], upP[:, c, 2 + HALF:], ALU.mult)
                    nc.vector.tensor_tensor(upS[:, c, :, 2:6],
                                            src[:, 1, SEQ - HALF:HALF].rearrange("p (n t) -> p n t", t=TDEC),
                                            upS[:, c, :, 2:6], ALU.mult).then_inc(zev_dve, 1)
                else:
                    c = n - 14
                    dve.wait_ge(conv_step, conv_done[c])
                    v = cv[:, c, :].rearrange("p (b n) -> p b n", b=2)
                    nc.vector.tensor_tensor(v, src, v, ALU.mult).then_inc(zev_dve, 1)

            def conv(c):
                dve.wait_ge(zev_dve, c + 1)
                if c == 0:
                    dve.wait_ge(zero_done, 3)
                    dve.wait_ge(pre_dve, 2)
                cp, cs = cv[:, c, 0:SEQ], cv[:, c, SEQ:T].rearrange("p (n t) -> p n t", t=TDEC)
                for j in range(3):
                    if j:
                        dve.wait_ge(conv_step, steps[0])
                    w = cwT[:, j, c:c + 1]
                    up, us = upP[:, c, j:j + SEQ], upS[:, c, :, j:j + TDEC]
                    if j == 0:
                        nc.vector.tensor_scalar(cp, up, w, None, ALU.mult)
                        nc.vector.tensor_scalar(cs, us, w, None, ALU.mult).then_inc(conv_step, 1)
                    else:
                        nc.vector.scalar_tensor_tensor(out=cp, in0=up, scalar=w, in1=cp, op0=ALU.mult, op1=ALU.add)
                        nc.vector.scalar_tensor_tensor(out=cs, in0=us, scalar=w, in1=cs, op0=ALU.mult, op1=ALU.add)\
                          .then_inc(conv_step, 1)
                    steps[0] += 1
                conv_done.append(steps[0])
                if c == CT - 1:
                    nc.vector.tensor_copy(cst[:, :, 0:2], upP[:, :, SEQ:SEQ + 2])
                    nc.vector.tensor_copy(cst[:, :, 2:18].rearrange("p c (n j) -> p c n j", j=2), upS[:, :, :, 4:6])\
                      .then_inc(cst_done, 1)

            def query_low(n):
                dve.wait_ge(zev_act, n + 1)
                src = slot2(n % 2).rearrange("p (b n) -> p b n", b=2)
                nc.vector.tensor_tensor(qTl[:, n - 2, 0:HALF], src[:, 0, 0:HALF], qTh[:, n - 2, 0:HALF].bitcast(F32),
                                        ALU.subtract)
                nc.vector.tensor_tensor(qTl[:, n - 2, HALF:], src[:, 1, 0:SEQ - HALF], qTh[:, n - 2, HALF:].bitcast(F32),
                                        ALU.subtract).then_inc(q_low, 1)

            dve.wait_ge(k_high, 1)
            nc.vector.tensor_tensor(kTl[:], kvT[:, 0, 0:SEQ], kTh[:].bitcast(F32), ALU.subtract).then_inc(k_low, 1)
            split_mix(2)
            query_low(2)
            query_low(3)
            split_mix(3)
            query_low(4)
            query_low(5)
            split_mix(4)
            dve.wait_ge(zev_act, 6)
            dve.wait_ge(zero_done, 3)
            for g in range(2):
                ins = nc.vector.tensor_copy(
                    qbd[HD * g:HD * g + HD, :, 16 * g:16 * g + 16].rearrange("p n (j t) -> p j n t", t=TDEC),
                    qS[HD * g:HD * g + HD].rearrange("p j (n t) -> p j n t", t=TDEC))
            ins.then_inc(qbd_done, 1)
            soft_a(0)
            soft_b(0)
            split_mix(5)
            probs(0)
            mixed(0)
            soft_a(1)
            soft_b(1)
            z_mult(10)
            conv(0)
            probs(1)
            split_mix(6)
            z_mult(11)
            mixed(1)
            split_mix(7)
            soft_a(2)
            z_mult(12)
            conv(1)
            soft_b(2)
            conv(2)
            z_mult(13)
            probs(2)
            split_mix(8)
            conv(3)
            z_mult(14)
            mixed(2)
            soft_a(3)
            z_mult(15)
            soft_b(3)
            split_mix(9)
            z_mult(16)
            probs(3)
            z_mult(17)
            mixed(3)
            split_mix(10)

            def yc_low(c):
                dve.wait_ge(yc_h, c + 1)
                nc.vector.tensor_tensor(yTl[:, c, :], cv[:, c, :], yTh[:, c, :].bitcast(F32), ALU.subtract).then_inc(yc_l, 1)

            dve.wait_ge(at_sc, 5)
            dve.wait_ge(at_yl, 4)
            nc.vector.tensor_tensor(Ss[:], ps[:, 4, 0:320].rearrange("p (a n) -> p a n", a=2), biass[:], ALU.add)\
              .then_inc(at_dv, 1)
            dve.wait_ge(at_dv, 25)
            nc.vector.tensor_reduce(mx[:, 0:2], Ss[:], AX_X, ALU.max).then_inc(at_dv, 1)
            dve.wait_ge(at_dv, 26)
            nc.vector.tensor_scalar(mm[:, 0:2], mx[:, 0:2], SCALE, sinks_s[:, 0:1], ALU.mult, ALU.max).then_inc(at_dv, 1)
            dve.wait_ge(at_dv, 27)
            nc.vector.tensor_scalar(negm[:, 0:2], mm[:, 0:2], -1.0, None, ALU.mult).then_inc(at_dv, 1)
            dve.wait_ge(at_ex, 6)
            nc.vector.tensor_tensor(den[:, 0:2], den[:, 0:2], es[:, 0:2], ALU.add).then_inc(at_dv, 1)
            dve.wait_ge(at_dv, 29)
            nc.vector.reciprocal(rden[:, 0:2], den[:, 0:2]).then_inc(at_dv, 1)
            dve.wait_ge(at_dv, 30)
            for a in range(2):
                ins = nc.vector.tensor_scalar(Ss[:, a, :], Ss[:, a, :], rden[:, a:a + 1], None, ALU.mult)
            ins.then_inc(at_dv, 1)
            for c in range(CT):
                yc_low(c)
            dve.wait_ge(at_yh, 5)
            nc.vector.tensor_tensor(yTl[:, CT:2 * CT, SEQ:T].rearrange("p j (n t) -> p j n t", t=TDEC),
                                    ps[:, 7, 0:P].rearrange("p (n j t) -> p j n t", n=NSEQ, t=TDEC),
                                    yTh[:, CT:2 * CT, SEQ:T].bitcast(F32).rearrange("p j (n t) -> p j n t", t=TDEC),
                                    ALU.subtract).then_inc(at_yl, 1)
            for dp in range(PAIRS):
                c = Z_CHUNKS + 3 * dp
                split_mix(c + 2)
                if dp < PAIRS - 1:
                    split_mix(c + 3)
                else:
                    split_wo(0)
                    split_wo(1)
                for u in range(2):
                    d = 2 * dp + u
                    dve.wait_ge(tiles_done, tiles_after(c + 1) + u + 1)
                    dve.wait_ge(sig_g, 4 * dp + 4)
                    for r in range(2):
                        src = slot2(2 * u + r).rearrange("p (b n) -> p b n", b=2)[:, :, 0:HALF]
                        v = sg[:, u, r, :].rearrange("p (b n) -> p b n", b=2)
                        nc.vector.tensor_tensor(v, src, v, ALU.mult).then_inc(mg_step, 1)
                    dve.wait_ge(mg_step, 3 * d + 2)
                    nc.vector.tensor_tensor(sg[:, u, 0, :], sg[:, u, 0, :], sg[:, u, 1, :], ALU.add).then_inc(mg_step, 1)
                    dve.wait_ge(mg_h, d + 1)
                    nc.vector.tensor_tensor(mTl[:, d, :], sg[:, u, 0, :], mTh[:, d, :].bitcast(F32), ALU.subtract)\
                      .then_inc(mg_l, 1)
                    if u == 0 and dp < PAIRS - 1:
                        split_mix(c + 4)
            split_wo(2)
            split_wo(3)
            nc.vector.memset(lg[:], 0.0).then_inc(r_step, 1)
            nc.vector.memset(mask[:], 0.0).then_inc(r_step, 1)
            nc.vector.memset(before[:], 0.0).then_inc(r_step, 1)
            nc.vector.memset(tabE[:], 0).then_inc(r_step, 1)
            nc.vector.memset(tabB[:], 0).then_inc(r_step, 1)
            dve.wait_ge(r_step, R0S)
            dve.wait_ge(xr_in, 32)
            dve.wait_ge(r_in, 48)
            dve.wait_ge(rc_in, 16 * 5)

            def add_out(i):
                r = ROWS[i]
                dve.wait_ge(tiles_done, TB - NT + i + 1)
                nc.vector.tensor_tensor(hrow[0:r, i, :], slot2(i % 2)[0:r, :], hrow[0:r, i, :], ALU.add).then_inc(wo_ev, 1)

            def m_rows(i):
                r = ROWS[i]
                dve.wait_ge(std_done, NT + i + 1)
                nc.vector.reciprocal(rinv[0:r, i:i + 1], std[0:r, i:i + 1]).then_inc(rinv_done, 1)
                dve.wait_ge(rinv_done, NT + i + 1)
                nc.vector.scalar_tensor_tensor(out=mrow[0:r, i, :], in0=hrow[0:r, i, :], scalar=rinv[0:r, i:i + 1],
                                               in1=gffn[0:r, :], op0=ALU.mult, op1=ALU.mult).then_inc(m_done, 1)

            def route(i):
                r, b = ROWS[i], R0S + ROUT * i
                dve.wait_ge(lg_mm, i + 1)
                nc.vector.tensor_tensor(lg[0:r, i, :], ps[0:r, 6 + i % 2, 0:NEXP], brt[0:r, :], ALU.add)\
                  .then_inc(r_step, 1)
                dve.wait_ge(r_step, b + 1)
                nc.vector.max(out=top[:, i, :], in_=lg[:, i, :]).then_inc(r_step, 1)
                dve.wait_ge(r_step, b + 2)
                nc.vector.tensor_tensor(ev[:, i, :], top[:, i, 0:TOPK], top[:, i, 0:1].broadcast_to([P, TOPK]), ALU.subtract)\
                  .then_inc(r_step, 1)
                nc.vector.max_index(out=topi[:, i, :], in_max=top[:, i, :], in_values=lg[:, i, :]).then_inc(r_step, 1)
                dve.wait_ge(r_step, b + 4)
                nc.vector.tensor_copy(topf[:, i, :], topi[:, i, 0:TOPK]).then_inc(r_step, 1)
                dve.wait_ge(r_step, b + 5)
                one = oneh[:, TOPK * i:TOPK * i + TOPK, :]
                nc.vector.tensor_tensor(one, io32[:].unsqueeze(1).broadcast_to([P, TOPK, NEXP]),
                                        topf[:, i, :].unsqueeze(2).broadcast_to([P, TOPK, NEXP]), ALU.is_equal)\
                  .then_inc(r_step, 1)
                dve.wait_ge(r_step, b + 6)
                nc.vector.tensor_reduce(mask[0:r, i, :], one[0:r].rearrange("p k e -> p e k"), AX_X, ALU.add).then_inc(r_step, 1)
                dve.wait_ge(r_step, b + 7)
                if i < NT - 1:
                    nc.vector.tensor_tensor(before[:, i + 1, :], before[:, i, :], mask[:, i, :], ALU.add).then_inc(r_step, 1)
                else:
                    nc.vector.tensor_tensor(all4[:], before[:, i, :].unsqueeze(1).broadcast_to([P, 4, NEXP]),
                                            mask[:, i, :].unsqueeze(1).broadcast_to([P, 4, NEXP]), ALU.add).then_inc(r_step, 1)

            for i in range(NT):
                add_out(i)
                if i == NT - 1:
                    route(NT - 3)
                m_rows(i)
                if 2 <= i < NT - 1:
                    route(i - 2)
            route(NT - 2)
            route(NT - 1)
            b = R0S + ROUT * NT
            dve.wait_ge(r_exp, 1)
            nc.vector.tensor_reduce(esum[:], ev[:], AX_X, ALU.add).then_inc(r_step, 1)
            dve.wait_ge(r_step, b + 1)
            nc.vector.reciprocal(ersum[:], esum[:]).then_inc(r_step, 1)
            dve.wait_ge(r_step, b + 2)
            nc.vector.tensor_tensor(ev[:], ev[:], ersum[:].unsqueeze(2).broadcast_to([P, NT, TOPK]), ALU.mult).then_inc(r_step, 1)
            dve.wait_ge(r_step, b + 3)
            nc.vector.tensor_tensor(oneh[:], oneh[:],
                                    ev[:].rearrange("p i k -> p (i k)").unsqueeze(2).broadcast_to([P, NT * TOPK, NEXP]),
                                    ALU.mult).then_inc(r_step, 1)
            dve.wait_ge(rk_mm, 1)
            nc.vector.tensor_tensor(over[:, 0:1], ps[:, 1, 0:1], code[:, 1:2], ALU.is_gt).then_inc(r_step, 1)
            nc.vector.scalar_tensor_tensor(out=rankm[:], in0=ps[:, 0, 0:NT * NEXP].rearrange("p (i e) -> p i e", e=NEXP),
                                           scalar=1.0, in1=mask[:], op0=ALU.add, op1=ALU.mult).then_inc(r_step, 1)
            dve.wait_ge(r_step, b + 4)
            nc.vector.tensor_reduce(gate[:], oneh[:].rearrange("p (i k) e -> p i e k", k=TOPK), AX_X, ALU.add)\
              .then_inc(r_step, 1)
            dve.wait_ge(r_step, b + 6)
            dve.wait_ge(io_in, 16)
            nc.vector.tensor_tensor(Rsel[:], iota[:, 0:P].unsqueeze(1).broadcast_to([P, NT, P]),
                                    rankm[:, :, 0:1].broadcast_to([P, NT, P]), ALU.is_equal).then_inc(sel0, 1)
            dve.wait_ge(r_step, b + 7)
            nc.vector.tensor_copy(V[:, :, 2:3], gate[:, :, 0:1]).then_inc(sel0, 1)
            dve.wait_ge(rk_mm, 2)
            nc.vector.tensor_copy(pos[:], ps[:, 2, 0:1]).then_inc(r_step, 1)
            dve.wait_ge(r_step, b + 8)
            nc.vector.tensor_scalar(oh16[:], io16[:], pos[:, 0:1], over[:, 0:1], ALU.is_equal, ALU.mult).then_inc(r_step, 1)
            nc.vector.tensor_copy(tabE[:, 0:NEXP], io32[0:1, :])
            dve.wait_ge(rk_mm, 3)
            nc.vector.tensor_copy(tabE[:, NEXP:NEXP + MAXOVER], ps[0:1, 3, 0:MAXOVER])
            nc.vector.tensor_copy(tabB[:, NEXP:NEXP + MAXOVER], ps[0:1, 3, 32:32 + MAXOVER])
            nc.vector.tensor_scalar(tabN[:, 0:1], ps[0:1, 3, 64:65], float(NEXP), None, ALU.add)
            nc.vector.tensor_scalar(tabN[:, 1:2], ps[0:1, 3, 64:65], float(NEXP - PEEL), None, ALU.add).then_inc(tab_done, 1)

            def split_pro(m):
                split(NM + m + 1, pro_slot(m), (m + 1) % SPL)

            def split_body(i, l):
                split(NM + 12 * i - 4 + l + 1, l % RAW, l % SPL)

            def rows_low(b):
                dve.wait_ge(xh_done, b + 1)
                nc.vector.tensor_tensor(xTl[:].rearrange("p k n -> p (k n)"), slot2(3),
                                        xTh[:].bitcast(F32).rearrange("p k n -> p (k n)"), ALU.subtract).then_inc(xl_done, 1)

            def clamp(i, hf, up_done):
                dve.wait_ge(tiles_done, up_done)
                if hf == 0:
                    dve.wait_ge(act_rows, 2 * i)
                src = ps[:, 2 * hf:2 * hf + 2, :].rearrange("p b (n t) -> p (b n) t", t=2)
                nc.vector.tensor_scalar(gl[:, 0, 512 * hf:512 * hf + 512], src[:, :, 0], LIMIT, None, ALU.min)
                nc.vector.tensor_scalar(gl[:, 1, 512 * hf:512 * hf + 512], src[:, :, 1], LIMIT, -LIMIT, ALU.min, ALU.max)\
                  .then_inc(gl_done, 1)

            def swiglu(i, hf):
                dve.wait_ge(gl_done, 2 * i + hf + 1)
                a = arow[:, 512 * hf:512 * hf + 512]
                nc.vector.scalar_tensor_tensor(out=a, in0=gl[:, 1, 512 * hf:512 * hf + 512], scalar=1.0,
                                               in1=gl[:, 0, 512 * hf:512 * hf + 512], op0=ALU.add, op1=ALU.mult)\
                  .then_inc(u_done, 1)
                dve.wait_ge(u_done, 2 * i + hf + 1)
                dve.wait_ge(sig_done, 2 * i + hf + 1)
                nc.vector.tensor_tensor(a, a, sgm[:, 512 * hf:512 * hf + 512], ALU.mult).then_inc(act_rows, 1)

            def act_low(i):
                dve.wait_ge(ah_done, i + 1)
                nc.vector.tensor_tensor(acTl[:].rearrange("p k n -> p (k n)"), slot2(3),
                                        acTh[:].bitcast(F32).rearrange("p k n -> p (k n)"), ALU.subtract).then_inc(al_done, 1)

            TB8 = TB + UPC
            split_pro(0)
            split_pro(1)
            split_pro(2)
            rows_low(0)
            for m in range(3, 8):
                split_pro(m)
            split_body(1, 0)
            split_body(1, 1)
            clamp(0, 0, TB8)
            clamp(0, 1, TB8)
            rows_low(1)
            split_body(1, 2)

            def body(i, first):
                for l in range(BLK):
                    if not (first and l < 3):
                        split_body(i, l)
                    if l == (2 if first else 0):
                        swiglu(i - 1, 0)
                    if l == (3 if first else 1):
                        swiglu(i - 1, 1)
                    if l == 6:
                        act_low(i - 1)
                    if l == 10:
                        rows_low(i + 1)
                        clamp(i, 0, TB + 12 * i + 4)
                clamp(i, 1, TB + 12 * i + 4)

            body(1, True)
            body(2, False)
            end = dve.value_load(tabN[0:1, 0:1], min_val=NEXP, max_val=NEXP + MAXOVER)
            nb = dve.value_load(tabN[0:1, 1:2], min_val=NEXP - PEEL, max_val=NEXP + MAXOVER - PEEL) + PEEL
            with dve.Fori(PEEL, end) as i:
                body(i, False)
            swiglu(nb - 1, 0)
            swiglu(nb - 1, 1)
            split_body(nb, 0)
            for k in range(2):
                dve.wait_ge(th_done, NT + k + 1)
                nc.vector.tensor_tensor(pTl[:, k, :], slot2(k)[:, 0:T], pTh[:, k, :].bitcast(F32), ALU.subtract)\
                  .then_inc(tl_done, 1)
            act_low(nb - 1)
            for l in range(1, DNC):
                split_body(nb, l)

            def split_ple(g, hi, lo):
                dve.wait_ge(rounded, NM + 12 * nb + g + 1)
                nc.vector.tensor_tensor(lo[:], raw[(4 + g) % RAW][:], hi[:].bitcast(F32), ALU.subtract).then_inc(split_done, 1)

            split_ple(0, wh[1], wl[1])
            for g in range(3):
                split_ple(g + 1, gate_h[g], gate_l[g])

            def rinv_of(which, i):
                n, c, r = NORMS.index((which, i)), 0 if which == "in" else 1, ROWS[i]
                dve.wait_ge(std2, n + 1)
                nc.vector.reciprocal(rinvt[0:r, c, i:i + 1], stdt[0:r, c, i:i + 1]).then_inc(rinv2, 1)
                dve.wait_ge(rinv2, n + 1)
                return rinvt[0:r, c, i:i + 1]

            def n_rows(i):
                r = ROWS[i]
                scalar = rinv_of("in", i)
                if i >= 3:
                    dve.wait_ge(g_add, i - 2)
                nc.vector.scalar_tensor_tensor(out=xnb[0:r, i % 3, :], in0=hrow[0:r, i, :], scalar=scalar, in1=gple[0:r, :],
                                               op0=ALU.mult, op1=ALU.mult).then_inc(nrow, 1)

            def n_low(i):
                dve.wait_ge(nhi, i + 1)
                tok = slice(P * i, P * i + ROWS[i])
                nc.vector.tensor_tensor(nTl[:, :, tok], slot2(2)[:, 0:KT * ROWS[i]].rearrange("p (k n) -> p k n", k=KT),
                                        nTh[:, :, tok].bitcast(F32), ALU.subtract).then_inc(nlo, 1)

            dve.wait_ge(gf_in, 32)
            dve.wait_ge(pp_mm, NT)
            n_rows(0)
            n_rows(1)
            n_low(0)
            split_ple(4, gate_h[3], gate_l[3])
            n_rows(2)
            n_low(1)
            for i in range(NT):
                r = ROWS[i]
                xr, hr = xnb[0:r, i % 3, :], hrow[0:r, i, :]
                dve.wait_ge(g_sig, i + 1)
                nc.vector.tensor_tensor(xr, xr, pp[0:r, i, :], ALU.mult).then_inc(g_mul, 1)
                dve.wait_ge(g_mul, i + 1)
                nc.vector.tensor_tensor(hr, hr, xr, ALU.add).then_inc(g_add, 1)
                if i + 2 < NT:
                    n_low(i + 2)
                scalar = rinv_of("out", i)
                nc.vector.scalar_tensor_tensor(out=hr, in0=hr, scalar=scalar, in1=gfin[0:r, :],
                                               op0=ALU.mult, op1=ALU.mult).then_inc(o_done, 1)
                if i + 3 < NT:
                    n_rows(i + 3)

        @block.tensor
        def _(pe):
            mmul = nc.tensor.matmul

            def three(out, ah, al, bh, bl, first, last):
                mmul(out, ah, bh, start=first, stop=False)
                mmul(out, ah, bl, start=False, stop=False)
                return mmul(out, al, bh, start=False, stop=last)

            def transpose_tiles(src, k, slot, width):
                for i in range(NT):
                    r = ROWS[i]
                    ins = nc.tensor.transpose(slot2(slot)[:, P * i:P * i + r], src[0:r, i, P * k:P * k + P], ident[0:r, 0:r])
                return ins

            pe.wait_ge(g_in, 32)
            for i in range(NT):
                r = ROWS[i]
                pe.wait_ge(xn_done, i + 1)
                if i >= 3:
                    pe.wait_ge(tl_done, i - 2)
                for k in range(KT):
                    ins = nc.tensor.transpose(slot2(i % 3)[:, r * k:r * k + r], xin[0:r, i, P * k:P * k + P], ident[0:r, 0:r])
                ins.then_inc(tr_done, 1)
            def project(c, slots, tiles=(0, 1)):
                pe.wait_ge(split_done, c + 1)
                s = c % SPL_MIX
                w_h = wh[s][:].rearrange("p (k n) -> p k n", k=KT)
                w_l = wl[s][:].rearrange("p (k n) -> p k n", k=KT)
                for u in tiles:
                    slots(u)
                    out = slot2(slot_of(c, u))
                    for k in range(KT):
                        lh, ll = w_h[:, k, P * u:P * u + P], w_l[:, k, P * u:P * u + P]
                        for w, a in ((lh, aTh), (lh, aTl), (ll, aTh)):
                            for b in range(2):
                                ins = mmul(out[:, 512 * b:512 * b + HALF], w, a[:, k, HALF * b:HALF * b + HALF],
                                           start=(k == 0 and a is aTh and w is lh),
                                           stop=(k == KT - 1 and w is ll), skip_group_check=False)
                    ins.then_inc(tiles_done, 1)

            def slot_of(c, u):
                if c < Z_CHUNKS:
                    return (2 * c + u) % 2
                return 2 * ((c - Z_CHUNKS) % 3) + u

            def z_free(c):
                def wait(u):
                    n = 2 * c + u - 2
                    if n < 0:
                        pe.wait_ge(tl_done, NT)
                    elif n < 10:
                        pe.wait_ge(zev_act, n + 1)
                        if 2 <= n < 6:
                            pe.wait_ge(q_low, n - 1)
                    else:
                        pe.wait_ge(zev_dve, n - 10 + 1)
                return wait

            def scores(n):
                if n == 0:
                    pe.wait_ge(zev_act, 6)
                    pe.wait_ge(pre_act, 3)
                    pe.wait_ge(q_low, 4)
                    pe.wait_ge(k_low, 1)
                lo = WIN if n == 0 else 0
                for h in (*range(2, NH), 0, 1):
                    if h == 0 and n:
                        pe.wait_ge(at_yl, n)
                    g, j = h // GRP, h % GRP
                    half, tok = slice(HD * g, HD * g + HD), slice(P * n, P * n + P)
                    keys = slice(P * (n - 1) + lo, P * (n + 1))
                    ins = three(ps[:, 4 + h // 2, 256 * (h % 2) + lo:256 * (h % 2) + 256], qTh[half, j, tok],
                                qTl[half, j, tok], kTh[half, keys], kTl[half, keys], True, True)
                ins.then_inc(at_sc, 1)

            def turn(n):
                pe.wait_ge(at_dv, 6 * n + 6)
                lo = 1 if n == 0 else 0
                for h in range(NH):
                    for kt in range(lo, 2):
                        ins = nc.tensor.transpose(ps[:, 4 + h // 2, 256 * (h % 2) + P * kt:256 * (h % 2) + P * kt + P],
                                                  S[:, h, P * kt:P * kt + P], ident[:])
                ins.then_inc(at_tr, 1)

            def values(n):
                lo = 1 if n == 0 else 0
                pe.wait_ge(at_ea, n + 1)
                pe.wait_ge(at_ed, n + 1)
                for g in range(NKV):
                    for j in range(GRP):
                        h = GRP * g + j
                        for kt in range(lo, 2):
                            ins = mmul(ps[HD * g:HD * g + HD, 4, P * j:P * j + P],
                                       vrow[:, n - 1 + kt, HD * g:HD * g + HD], PT[:, 2 * h + kt, :],
                                       start=(kt == lo), stop=(kt == 1))
                ins.then_inc(at_pv, 1)

            def sample_scores():
                pe.wait_ge(at_yl, 4)
                pe.wait_ge(qbd_done, 1)
                for n in range(NSEQ):
                    a, r = n // 4, 32 * (n % 4)
                    mmul(ps[r:r + 32, 4, 160 * a:160 * a + P], qbd[:, n, :], ksT[:, n, :], start=True, stop=True)
                    ins = mmul(ps[r:r + 32, 4, 160 * a + P:160 * a + 160], qbd[:, n, :], kvT[:, 0, SEQ:T],
                               start=True, stop=True)
                ins.then_inc(at_sc, 1)

            def sample_turn():
                pe.wait_ge(at_dv, 31)
                for a in range(2):
                    nc.tensor.transpose(ps[:, 5, P * a:P * a + P], Ss[:, a, 0:P], ident[:])
                    ins = nc.tensor.transpose(ps[0:TS, 6, P * a:P * a + P], Ss[:, a, P:160], ident[:])
                ins.then_inc(at_tr, 1)

            def sample_values():
                pe.wait_ge(at_ea, 5)
                pe.wait_ge(vc_in, 16)
                for n in range(NSEQ):
                    a = n // 4
                    for g in range(NKV):
                        out = ps[HD * g:HD * g + HD, 7, 16 * n:16 * n + 16]
                        col = slice(32 * (n % 4) + 16 * g, 32 * (n % 4) + 16 * g + 16)
                        mmul(out, vc[:, n, HD * g:HD * g + HD], PsT[:, a, col], start=True, stop=False)
                        ins = mmul(out, vrow[0:TS, 4, HD * g:HD * g + HD], PsN[:, a, col], start=False, stop=True)
                ins.then_inc(at_pv, 1)

            def new_rows():
                pe.wait_ge(zev_act, 2)
                pe.wait_ge(pre_act, 1)
                pe.wait_ge(pre_dve, 2)
                for i in range(4):
                    nc.tensor.transpose(ps[:, 4, P * i:P * i + P], kvT[:, 1, P * i:P * i + P], ident[:])
                nc.tensor.transpose(ps[0:TS, 5, 0:P], kvT[:, 1, SEQ:T], ident[:])
                nc.tensor.transpose(ps[:, 5, P:2 * P], kvT[:, 0, SEQ - WIN:SEQ], ident[:])
                nc.tensor.transpose(ps[0:TS, 5, 2 * P:3 * P], kvT[:, 0, SEQ:T], ident[:]).then_inc(pre_pe, 1)

            project(0, z_free(0))
            pe.wait_ge(st_in, 16)
            for c in range(CT):
                ins = nc.tensor.transpose(ps[:, 4, 16 * c:16 * c + 16], strow[:, P * c:P * c + P], ident[0:16, 0:16])
            ins.then_inc(pre_pe, 1)
            pe.wait_ge(ck_in, 16)
            for n in range(NSEQ):
                ins = nc.tensor.transpose(ps[:, 5 + n // 4, P * (n % 4):P * (n % 4) + P], ckrow[:, n, :], ident[:])
            ins.then_inc(pre_pe, 1)
            project(1, z_free(1))
            new_rows()
            project(2, z_free(2))

            def half(n):
                project(n // 2, z_free(n // 2), (n % 2,))

            n = 6
            for b in range(4):
                scores(b)
                half(n)
                half(n + 1)
                turn(b)
                half(n + 2)
                values(b)
                n += 3
            sample_scores()
            c = Z_CHUNKS

            def gate_free(dp, r):
                def wait(u):
                    if dp == 0:
                        pe.wait_ge(zev_dve, 2 * CT)
                        if r == 1:
                            pe.wait_ge(at_yl, 5)
                            pe.wait_ge(crow_done, 1)
                    else:
                        pe.wait_ge(mg_step, 3 * (2 * dp - 2 + r) + 3)
                return wait

            project(c, gate_free(0, 0), (0,))
            sample_turn()
            project(c, gate_free(0, 0), (1,))
            sample_values()
            pe.wait_ge(cst_done, 1)
            for c in range(CT):
                ins = nc.tensor.transpose(ps[0:18, 4, P * c:P * c + P], cst[:, c, :], ident[:])
            ins.then_inc(cst_tr, 1)

            for dp in range(PAIRS):
                c = Z_CHUNKS + 3 * dp

                if dp > 0:
                    project(c, gate_free(dp, 0))
                project(c + 1, gate_free(dp, 1))
                pe.wait_ge(split_done, c + 3)
                if dp == 0:
                    pe.wait_ge(yc_l, CT)
                    pe.wait_ge(at_yl, 5)
                s = (c + 2) % SPL_MIX
                w_h = wh[s][:].rearrange("p (k n) -> p k n", k=KT)
                w_l = wl[s][:].rearrange("p (k n) -> p k n", k=KT)
                for u in range(2):
                    pe.wait_ge(sig_g, 4 * dp + 2 * (u + 1))
                    for r in range(2):
                        out = slot2(2 * u + r)
                        for k in range(CT):
                            lh, ll = w_h[:, CT * r + k, P * u:P * u + P], w_l[:, CT * r + k, P * u:P * u + P]
                            for w, y in ((lh, yTh), (lh, yTl), (ll, yTh)):
                                for b in range(2):
                                    ins = mmul(out[:, 512 * b:512 * b + HALF], w, y[:, CT * r + k, HALF * b:HALF * b + HALF],
                                               start=(k == 0 and w is lh and y is yTh), stop=(k == CT - 1 and w is ll))
                    ins.then_inc(tiles_done, 1)

            def out_rows(i):
                r = ROWS[i]
                tok = slice(P * i, P * i + r)
                if i >= 2:
                    pe.wait_ge(wo_ev, i - 1)
                order = [(g, k) for g in range(WO_CHUNKS) for k in range(KT)]
                if i == 0:
                    pe.wait_ge(mg_step, 3 * (KT - 2) + 2)
                    order.sort(key=lambda gk: (gk[0] >= 2, max(gk[1] - KT + 3, 0) if gk[0] < 2 else gk[0]))
                seen = 0
                for n, (g, k) in enumerate(order):
                    if i == 0:
                        if k + 1 > seen:
                            pe.wait_ge(mg_l, k + 1)
                            seen = k + 1
                        if k == 0:
                            pe.wait_ge(split_done, Z_CHUNKS + BR_CHUNKS + g + 1)
                    w_h = wo_h[g][:].rearrange("p (k n) -> p k n", k=KT)
                    w_l = wo_l[g][:].rearrange("p (k n) -> p k n", k=KT)
                    col = 256 * WO_COL[g]
                    ins = three(slot2(i % 2)[0:r, col:col + 256], mTh[:, k, tok], mTl[:, k, tok],
                                w_h[:, k, :], w_l[:, k, :], k == 0, k == KT - 1)
                ins.then_inc(tiles_done, 1)

            def m_turn(i):
                pe.wait_ge(m_done, i + 1)
                if i:
                    pe.wait_ge(mtr_ev, i)
                r = ROWS[i]
                for k in range(KT):
                    ins = nc.tensor.transpose(slot2(2)[:, r * k:r * k + r], mrow[0:r, i, P * k:P * k + P], ident[0:r, 0:r])
                ins.then_inc(mtr, 1)

            def logits(i):
                pe.wait_ge(mtr_ev, i + 1)
                if i >= 2:
                    pe.wait_ge(r_step, R0S + ROUT * (i - 2) + 1)
                r = ROWS[i]
                for k in range(KT):
                    ins = mmul(ps[0:r, 6 + i % 2, 0:NEXP], mTf[:, i % 2, r * k:r * k + r], wr[:, k, :],
                               start=(k == 0), stop=(k == KT - 1))
                ins.then_inc(lg_mm, 1)

            out_rows(0)
            out_rows(1)
            m_turn(0)
            pe.wait_ge(r_in, 48)
            for i in range(2, NT):
                out_rows(i)
                logits(i - 2)
                m_turn(i - 1)
            logits(NT - 2)
            m_turn(NT - 1)
            logits(NT - 1)
            pe.wait_ge(r_step, R0S + ROUT * NT)
            pe.wait_ge(rc_in, 16 * 5)
            mmul(ps[:, 1, 0:1], all4[:].rearrange("p b e -> p (b e)"), ones[:, 0:1], start=True, stop=True)
            out = ps[:, 0, 0:NT * NEXP]
            mmul(out, tri[:], mask[:].rearrange("p i e -> p (i e)"), start=True, stop=False)
            mmul(out, ones[:], before[:].rearrange("p i e -> p (i e)"), start=False, stop=True).then_inc(rk_mm, 1)
            pe.wait_ge(r_step, R0S + ROUT * NT + 5)
            mmul(ps[:, 2, 0:1], tri[:], over[:, 0:1], start=True, stop=True).then_inc(rk_mm, 1)

            def disp(b):
                if isinstance(b, int) and b == 0:
                    pe.wait_ge(sel0, 2)
                else:
                    pe.wait_ge(rv_done, b)
                for i in range(NT):
                    ins = mmul(ps[:, 6, 0:3], Rsel[:, i, :], V[:, i, :], start=(i == 0), stop=(i == NT - 1))
                ins.then_inc(disp_mm, 1)

            def tx(b):
                pe.wait_ge(gathered, 16 * b + 16)
                for k in range(KT):
                    ins = nc.tensor.transpose(slot2(3)[:, P * k:P * k + P], xg[:, P * k:P * k + P], ident[:])
                ins.then_inc(tx_done, 1)

            def ta(i):
                pe.wait_ge(act_rows, 2 * i + 2)
                for k in range(KT):
                    ins = nc.tensor.transpose(slot2(3)[:, P * k:P * k + P], arow[:, P * k:P * k + P], ident[:])
                ins.then_inc(ta_done, 1)

            def up_chunk(k, slot):
                if k == 0:
                    for n in range(4):
                        mmul(ps[:, n, :], one2[:], bup[:, 512 * n:512 * n + 512], start=True, stop=False)
                for x, w in ((xTh, wh), (xTh, wl), (xTl, wh)):
                    for n in range(4):
                        ins = mmul(ps[:, n, :], x[:, k, :], w[slot][:, 512 * n:512 * n + 512], start=False,
                                   stop=(k == UPC - 1 and x is xTl))
                ins.then_inc(tiles_done, 1)

            def down_chunk(c, slot):
                if c == 0:
                    for n in range(2):
                        mmul(ps[:, 4 + n, :], one2[:], bdn[:, 512 * n:512 * n + 512], start=True, stop=False)
                for j in range(2):
                    for a, w in ((acTh, wh), (acTh, wl), (acTl, wh)):
                        for n in range(2):
                            ins = mmul(ps[:, 4 + n, :], a[:, 2 * c + j, :], w[slot][:, D * j + 512 * n:D * j + 512 * n + 512],
                                       start=False, stop=(c == DNC - 1 and j == 1 and a is acTl))
                ins.then_inc(tiles_done, 1)

            disp(0)
            pe.wait_ge(r_step, R0S + ROUT * NT + 9)
            mmul(ps[0:1, 3, 0:MAXOVER], code[:, 0:1], oh16[:], start=True, stop=True)
            mmul(ps[0:1, 3, 32:32 + MAXOVER], code[:, 1:2], oh16[:], start=True, stop=True)
            mmul(ps[0:1, 3, 64:65], ones[:, 0:1], over[:, 0:1], start=True, stop=True).then_inc(rk_mm, 1)
            pe.wait_ge(disp_cp, 1)
            tx(0)
            pe.wait_ge(tab_done, 1)
            pe.wait_ge(b_rnd, 2)
            for k in range(UPC):
                pe.wait_ge(split_done, NM + k + 1)
                if k == 0:
                    pe.wait_ge(bup_in, 16)
                    pe.wait_ge(xl_done, 1)
                up_chunk(k, (k + 1) % SPL)
                if k == 0:
                    disp(1)
                if k == 7:
                    pe.wait_ge(disp_cp, 2)
                    tx(1)

            def body(i, first):
                for l in range(UPC):
                    pe.wait_ge(split_done, NM + 12 * i - 4 + l + 1)
                    if l == 0:
                        pe.wait_ge(bup_in, 16 * i + 16)
                        pe.wait_ge(gl_done, 2 * i)
                        pe.wait_ge(xl_done, i + 1)
                    up_chunk(l, l % SPL)
                    if l == 0:
                        disp(i + 1)
                    if l == 3:
                        pe.wait_ge(disp_cp, i + 2)
                        ta(i - 1)
                    if l == 7:
                        pe.wait_ge(al_done, i)
                        tx(i + 1)
                for l in range(UPC, BLK):
                    pe.wait_ge(split_done, NM + 12 * i - 4 + l + 1)
                    if l == UPC:
                        pe.wait_ge(bdn_in, 16 * i)
                        if not first:
                            pe.wait_ge(y_done, i - 1)
                    down_chunk(l - UPC, l % SPL)

            body(1, True)
            body(2, False)
            end = pe.value_load(tabN[0:1, 0:1], min_val=NEXP, max_val=NEXP + MAXOVER)
            nb = pe.value_load(tabN[0:1, 1:2], min_val=NEXP - PEEL, max_val=NEXP + MAXOVER - PEEL) + PEEL
            with pe.Fori(PEEL, end) as i:
                body(i, False)
            pe.wait_ge(gl_done, 2 * nb)
            pe.wait_ge(p_in, 32)
            for k in range(2):
                transpose_tiles(prow, k, k, T).then_inc(tr_done, 1)
            pe.wait_ge(xl_done, nb + 1)
            ta(nb - 1)
            pe.wait_ge(al_done, nb)
            pe.wait_ge(bdn_in, 16 * nb)
            pe.wait_ge(y_done, nb - 1)
            for l in range(DNC):
                pe.wait_ge(split_done, NM + 12 * nb - 4 + l + 1)
                down_chunk(l, l % SPL)
            pe.wait_ge(split_done, NM + 12 * nb + 1)
            pe.wait_ge(tl_done, NT + 2)
            w_h = wh[1][:].rearrange("p (k n) -> p k n", k=2)
            w_l = wl[1][:].rearrange("p (k n) -> p k n", k=2)
            for i in range(NT):
                r = ROWS[i]
                if i >= 3:
                    pe.wait_ge(pp_ev, i - 2)
                for n in range(2):
                    for k in range(2):
                        tok, col = slice(P * i, P * i + r), slice(512 * n, 512 * n + 512)
                        ins = three(ps[0:r, 2 * PP_SLOT[i] + n, :], pTh[:, k, tok], pTl[:, k, tok], w_h[:, k, col],
                                    w_l[:, k, col], k == 0, k == 1)
                ins.then_inc(pp_mm, 1)

            def n_turn(i):
                pe.wait_ge(nrow, i + 1)
                if i:
                    pe.wait_ge(nlo, i)
                else:
                    pe.wait_ge(y_done, nb)
                r = ROWS[i]
                for k in range(KT):
                    ins = nc.tensor.transpose(slot2(2)[:, r * k:r * k + r], xnb[0:r, i % 3, P * k:P * k + P], ident[0:r, 0:r])
                ins.then_inc(ntr, 1)

            def gates_of(i):
                r = ROWS[i]
                pe.wait_ge(nlo, i + 1)
                if i < 2:
                    pe.wait_ge(pp_ev, NT)
                else:
                    pe.wait_ge(g_sig, i - 1)
                for g in range(4):
                    if i == 0:
                        pe.wait_ge(split_done, NM + 12 * nb + 1 + g + 1)
                    w_h = gate_h[g][:].rearrange("p (k n) -> p k n", k=KT)
                    w_l = gate_l[g][:].rearrange("p (k n) -> p k n", k=KT)
                    for k in range(KT):
                        tok = slice(P * i, P * i + r)
                        ins = three(slot2(i % 2)[0:r, 256 * g:256 * g + 256], nTh[:, k, tok], nTl[:, k, tok],
                                    w_h[:, k, :], w_l[:, k, :], k == 0, k == KT - 1)
                ins.then_inc(g_mm, 1)

            n_turn(0)
            n_turn(1)
            for i in range(NT):
                gates_of(i)
                if i + 2 < NT:
                    n_turn(i + 2)


OUTS = {
    "y_prompt": (1, SEQ, D), "y_sample": (NSEQ, TDEC, D), "conv_prompt": (1, 1, 2, CW), "conv_sample": (1, NSEQ, 2, CW),
    "k_prompt": (1, 1, WIN, NKV, HD), "v_prompt": (1, 1, WIN, NKV, HD),
    "k_sample": (1, NSEQ, WIN, NKV, HD), "v_sample": (1, NSEQ, WIN, NKV, HD),
}


def kernel(**inputs):
    import concourse.bacc as bacc
    from concourse.bass_utils import run_bass_kernel_spmd

    a = {k: np.asarray(v) for k, v in inputs.items()}
    arrays = {k: np.ascontiguousarray(a[k]) for k in (
        "x_prompt", "x_sample", "state_conv", "cache_k", "cache_v", "p_prompt", "p_sample", "sinks", "g_ffn",
        "g_mix", "g_ple", "w_router", "b_router", "w_up", "b_up", "w_down", "b_down", "g_final")}
    w_in, w_br, w_out = a["w_in"][0], a["w_branch"][0], a["w_out"][0]
    head = np.arange(NH * HD).reshape(NKV, GRP, HD).transpose(1, 0, 2).reshape(-1)
    q0, k0, g0 = 3 * CW, 3 * CW + NH * HD, 3 * CW + NH * HD + 2 * NKV * HD
    rng = np.arange(256)
    cols = [k0 + rng] + [q0 + head[:256], q0 + head[256:]] + [b + rng for b in (CW, CW + 256, 2 * CW, 2 * CW + 256, 0, 256)]

    def chunk(w, c):
        return w[:, c].reshape(KT, P, 256).transpose(1, 0, 2).reshape(P, CH)

    mix = [chunk(w_in, c) for c in cols]
    for dp in range(PAIRS):
        mix += [chunk(w_in, g0 + D * r + 256 * dp + rng) for r in range(2)]
        mix.append(chunk(np.concatenate([w_br[0], w_br[1][head]]), 256 * dp + rng))
    mix += [chunk(w_out, 256 * g + rng) for g in WO_COL]
    arrays["w_mix"] = np.ascontiguousarray(np.stack(mix))
    ple = [a["w_ple"][0].reshape(2, P, D).transpose(1, 0, 2).reshape(P, CH)]
    ple += [chunk(a["w_ple_gate"][0], 256 * g + rng) for g in range(4)]
    arrays["w_ple_chunks"] = np.ascontiguousarray(np.stack(ple))
    arrays["conv_cols"] = np.ascontiguousarray(a["conv_w"][0].reshape(3, CT, P).transpose(2, 0, 1))
    arrays["sink_rows"] = np.ascontiguousarray(np.tile(np.repeat(a["sinks"][0], TDEC), 4)[:, None])
    arrays |= constants()

    nc = bacc.Bacc("TRN2", target_bir_lowering=False, num_devices=1)
    A = {n: nc.dram_tensor(n, v.shape, mybir.dt.from_np(v.dtype), kind="ExternalInput").ap() for n, v in arrays.items()}
    O = {n: nc.dram_tensor(n, s, F32, kind="ExternalOutput").ap() for n, s in OUTS.items()}
    build(nc, A, O)
    r = run_bass_kernel_spmd(nc, [arrays], core_ids=[0])
    return tuple(r.results[0][n] for n in OUTS)


def constants():
    f = np.float32
    p, c = np.arange(P)[:, None], np.arange(256)[None, :]
    dist = p + WIN - c
    negd = np.where((dist >= 0) & (dist < WIN), -dist, -1e30)
    s4, h, t = p[:, 0] // 32, p[:, 0] % 32 // TDEC, p[:, 0] % TDEC
    slope = np.array(SLOPE)[h] / SCALE
    bias = np.full((P, 2, 160), -1e30)
    for a in range(2):
        for j in range(WIN):
            bias[:, a, j] = np.where(j > t, -(WIN + t - j) * slope, -1e30)
        for n in range(NSEQ):
            for u in range(TDEC):
                bias[:, a, WIN + TDEC * n + u] = np.where((4 * a + s4 == n) & (u <= t), -(t - u) * slope, -1e30)
    tok = np.zeros((P, NT, 3))
    tok[:, :, 0] = P * np.arange(NT)[None, :] + p
    tok[:, :, 1] = 1
    code = np.zeros((P, 3))
    code[:, 0] = p[:, 0] % NEXP
    code[:, 1] = P * (p[:, 0] // NEXP + 1)
    out = {
        "c_ident": np.eye(P), "c_negd": negd, "c_biass": bias, "c_tok": tok, "c_code": code,
        "c_tri": p < np.arange(P)[None, :], "c_ones": np.ones((P, P)),
        "c_pad": np.concatenate([-(T + p), T + p], 1),
        "c_io16": np.broadcast_to(np.arange(MAXOVER), (P, MAXOVER)), "c_io32": np.broadcast_to(np.arange(NEXP), (P, NEXP)),
        "c_iota": np.broadcast_to(1 + np.arange(NT * P), (P, NT * P)), "c_zero": np.zeros((P, D)),
    }
    return {k: np.ascontiguousarray(v.astype(f)) for k, v in out.items()}
```
